# Optimizing a Trainium2 kernel written in Bass

```python
import jax, jax.numpy as jnp
from jax import lax
import numpy as np

D_MODEL = 1024
BATCH = 1
SEQ = 1024
DEPTH = 1

GRID_W = 64
HEAD_DIM = 64
NA_HEADS = 8
NA_WIN_H = 8
NA_WIN_W = 16
GQA_HEADS = 8
GQA_KV_HEADS = 2
Q_BLOCK = 128
ROPE_THETA = 10000.0
N_EXPERTS = 16
EC_CAPACITY_FACTOR = 2
D_EXPERT = 2816
NORM_EPS = 1e-6

NA_WIDTH = NA_HEADS * HEAD_DIM
GQA_WIDTH = GQA_HEADS * HEAD_DIM
GQA_KV_WIDTH = GQA_KV_HEADS * HEAD_DIM
MIX_WIDTH = NA_WIDTH + GQA_WIDTH
IN_WIDTH = 3 * NA_WIDTH + GQA_WIDTH + 2 * GQA_KV_WIDTH

kernel_name = "hymba_natten_gqa_axialrope_expert_choice"

def rms_norm(x, g):
    xf = x.astype(jnp.float32)
    y = xf * lax.rsqrt(jnp.mean(xf * xf, axis=-1, keepdims=True) + NORM_EPS)
    return (y * g.astype(jnp.float32)).astype(x.dtype)

def neighbourhood_attention(q, k, v, rpb):
    B, S, H, D = q.shape
    rows = S // GRID_W
    kh = min(NA_WIN_H, rows)
    kw = NA_WIN_W
    n_nb = kh * kw
    qg = q.reshape(B, rows, GRID_W, H, D)
    kg = k.reshape(B, rows, GRID_W, H, D)
    vg = v.reshape(B, rows, GRID_W, H, D)
    row_start = jnp.clip(jnp.arange(rows) - kh // 2, 0, rows - kh)
    col = jnp.arange(GRID_W)
    col_start = jnp.clip(col - kw // 2, 0, GRID_W - kw)
    col_idx = col_start[:, None] + jnp.arange(kw)[None, :]
    col_off = col_idx - col[:, None] + (NA_WIN_W - 1)
    scale = D ** -0.5

    def one_row(r):
        rs = row_start[r]
        k_rows = lax.dynamic_slice_in_dim(kg, rs, kh, axis=1)
        v_rows = lax.dynamic_slice_in_dim(vg, rs, kh, axis=1)
        k_nb = k_rows[:, :, col_idx].transpose(0, 2, 1, 3, 4, 5).reshape(B, GRID_W, n_nb, H, D)
        v_nb = v_rows[:, :, col_idx].transpose(0, 2, 1, 3, 4, 5).reshape(B, GRID_W, n_nb, H, D)
        q_r = lax.dynamic_index_in_dim(qg, r, axis=1, keepdims=False)
        s = jnp.einsum('bwhd,bwnhd->bhwn', q_r, k_nb).astype(jnp.float32) * scale
        row_off = rs + jnp.arange(kh) - r + (NA_WIN_H - 1)
        bias = rpb[:, row_off[:, None, None], col_off[None, :, :]]
        bias = bias.transpose(0, 2, 1, 3).reshape(H, GRID_W, n_nb)
        p = jax.nn.softmax(s + bias[None].astype(jnp.float32), axis=-1).astype(v.dtype)
        return jnp.einsum('bhwn,bwnhd->bwhd', p, v_nb)

    o = lax.map(one_row, jnp.arange(rows))
    return o.transpose(1, 0, 2, 3, 4).reshape(B, S, H * D)

def axial_rope_tables(S):
    t = jnp.arange(S)
    row = (t // GRID_W).astype(jnp.float32)
    col = (t % GRID_W).astype(jnp.float32)
    half = HEAD_DIM // 2
    inv_freq = 1.0 / (ROPE_THETA ** (jnp.arange(0, half, 2, dtype=jnp.float32) / half))
    ang = jnp.concatenate([row[:, None] * inv_freq[None], col[:, None] * inv_freq[None]], axis=-1)
    return jnp.cos(ang), jnp.sin(ang)

def apply_rope(x, cos, sin):
    B, S, H, D = x.shape
    xf = x.astype(jnp.float32).reshape(B, S, H, D // 2, 2)
    x0, x1 = xf[..., 0], xf[..., 1]
    c = cos[None, :, None, :]
    s = sin[None, :, None, :]
    out = jnp.stack([x0 * c - x1 * s, x0 * s + x1 * c], axis=-1)
    return out.reshape(B, S, H, D).astype(x.dtype)

def gqa_attention(q, k, v):
    B, S, Hq, D = q.shape
    Hkv = k.shape[2]
    G = Hq // Hkv
    scale = D ** -0.5
    qb = q.reshape(B, S // Q_BLOCK, Q_BLOCK, Hkv, G, D).transpose(1, 0, 2, 3, 4, 5)

    def block(qi):
        s = jnp.einsum('bqkgd,bskd->bkgqs', qi, k).astype(jnp.float32) * scale
        p = jax.nn.softmax(s, axis=-1).astype(v.dtype)
        return jnp.einsum('bkgqs,bskd->bqkgd', p, v)

    o = lax.map(block, qb)
    return o.transpose(1, 0, 2, 3, 4, 5).reshape(B, S, Hq * D)

def expert_choice_ffn(h, w_router, w_gate, w_up, w_down):
    B, S, D = h.shape
    cap = EC_CAPACITY_FACTOR * S // N_EXPERTS
    logits = jnp.einsum('bsd,de->bse', h, w_router).astype(jnp.float32)
    affinity = jax.nn.softmax(logits, axis=-1)
    gate, idx = lax.top_k(affinity.transpose(0, 2, 1), cap)
    xin = jax.vmap(lambda hb, ib: hb[ib])(h, idx)
    g = jnp.einsum('becd,edf->becf', xin, w_gate)
    u = jnp.einsum('becd,edf->becf', xin, w_up)
    y = jnp.einsum('becf,efd->becd', jax.nn.silu(g) * u, w_down)
    y = y * gate[..., None].astype(y.dtype)
    return jax.vmap(
        lambda ib, yb: jnp.zeros((S, D), yb.dtype).at[ib.reshape(-1)].add(yb.reshape(-1, D))
    )(idx, y)

def setup_inputs(seed: int = 0) -> dict:
    key = jax.random.key(seed)
    ks = jax.random.split(key, 16)
    f32 = jnp.float32

    def nrm(k, shape, fan_in):
        return jax.random.normal(k, shape, f32) * (fan_in ** -0.5)

    def gain(k, shape):
        return 1.0 + 0.02 * jax.random.normal(k, shape, f32)

    return {
        "x": jax.random.normal(ks[0], (BATCH, SEQ, D_MODEL), f32),
        "norm1_g": gain(ks[1], (DEPTH, D_MODEL)),
        "w_in": nrm(ks[2], (DEPTH, D_MODEL, IN_WIDTH), D_MODEL),
        "na_q_norm_g": gain(ks[3], (DEPTH, HEAD_DIM)),
        "na_k_norm_g": gain(ks[4], (DEPTH, HEAD_DIM)),
        "na_rpb": 0.02 * jax.random.normal(ks[5], (DEPTH, NA_HEADS, 2 * NA_WIN_H - 1, 2 * NA_WIN_W - 1), f32),
        "gqa_q_norm_g": gain(ks[6], (DEPTH, HEAD_DIM)),
        "gqa_k_norm_g": gain(ks[7], (DEPTH, HEAD_DIM)),
        "na_out_g": gain(ks[8], (DEPTH, NA_WIDTH)),
        "gqa_out_g": gain(ks[9], (DEPTH, GQA_WIDTH)),
        "w_out": nrm(ks[10], (DEPTH, MIX_WIDTH, D_MODEL), MIX_WIDTH),
        "norm2_g": gain(ks[11], (DEPTH, D_MODEL)),
        "w_router": nrm(ks[12], (DEPTH, D_MODEL, N_EXPERTS), D_MODEL),
        "w_gate": nrm(ks[13], (DEPTH, N_EXPERTS, D_MODEL, D_EXPERT), D_MODEL),
        "w_up": nrm(ks[14], (DEPTH, N_EXPERTS, D_MODEL, D_EXPERT), D_MODEL),
        "w_down": nrm(ks[15], (DEPTH, N_EXPERTS, D_EXPERT, D_MODEL), D_EXPERT),
    }

def reference(x, norm1_g, w_in, na_q_norm_g, na_k_norm_g, na_rpb, gqa_q_norm_g, gqa_k_norm_g,
              na_out_g, gqa_out_g, w_out, norm2_g, w_router, w_gate, w_up, w_down):
    B, S, _ = x.shape
    cos, sin = axial_rope_tables(S)
    splits = np.cumsum([NA_WIDTH, NA_WIDTH, NA_WIDTH, GQA_WIDTH, GQA_KV_WIDTH]).tolist()
    for l in range(DEPTH):
        u = rms_norm(x, norm1_g[l])
        proj = jnp.einsum('bsd,dn->bsn', u, w_in[l])
        qa, ka, va, qb, kb, vb = jnp.split(proj, splits, axis=-1)
        qa = rms_norm(qa.reshape(B, S, NA_HEADS, HEAD_DIM), na_q_norm_g[l])
        ka = rms_norm(ka.reshape(B, S, NA_HEADS, HEAD_DIM), na_k_norm_g[l])
        va = va.reshape(B, S, NA_HEADS, HEAD_DIM)
        out_a = neighbourhood_attention(qa, ka, va, na_rpb[l])
        qb = rms_norm(qb.reshape(B, S, GQA_HEADS, HEAD_DIM), gqa_q_norm_g[l])
        kb = rms_norm(kb.reshape(B, S, GQA_KV_HEADS, HEAD_DIM), gqa_k_norm_g[l])
        vb = vb.reshape(B, S, GQA_KV_HEADS, HEAD_DIM)
        qb = apply_rope(qb, cos, sin)
        kb = apply_rope(kb, cos, sin)
        out_b = gqa_attention(qb, kb, vb)
        mixed = jnp.concatenate([rms_norm(out_a, na_out_g[l]), rms_norm(out_b, gqa_out_g[l])], axis=-1)
        x = x + jnp.einsum('bsm,md->bsd', mixed, w_out[l])
        hn = rms_norm(x, norm2_g[l])
        x = x + expert_choice_ffn(hn, w_router[l], w_gate[l], w_up[l], w_down[l])
    return x


_drawn_inputs = setup_inputs


def setup_inputs(seed=0):
    import zlib

    import numpy as np

    out = dict(_drawn_inputs(seed))
    spreads = {}
    factors = {'na_q_norm_g': 4.057,
     'na_k_norm_g': 4.495,
     'na_rpb': 4.453,
     'gqa_q_norm_g': 4.433,
     'gqa_k_norm_g': 4.316,
     'na_out_g': 4.292,
     'gqa_out_g': 4.527,
     'norm2_g': 4.942}
    for name, (base, spread) in spreads.items():
        noise = np.random.default_rng([zlib.crc32(name.encode()), seed]).standard_normal(out[name].shape)
        drawn = base * np.exp(spread * noise) if base else spread * noise
        out[name] = __import__('jax').numpy.asarray(drawn.astype(out[name].dtype))
    for name, factor in factors.items():
        out[name] = (out[name] * factor).astype(out[name].dtype)
    return out
```

```python
from contextlib import ExitStack

import concourse.bass as bass
import numpy as np
from concourse import mybir
from concourse.alu_op_type import AluOpType as ALU

ACT = mybir.ActivationFunctionType
AX = mybir.AxisListType.X
F32, F32R, U32 = mybir.dt.float32, mybir.dt.float32r, mybir.dt.uint32

P = 128
S = D = 1024
NT = S // P
KD = D // P
HD = 64
GRID_W = 64
NH = 8
KVH = 2
NQ0, NK0, NV0 = 0, 512, 1024
GQ0, GK0, GV0 = 1536, 2048, 2176
INW = 2304
GW = 256
NG = INW // GW
E, CAP, FE = 16, 128, 2816
EPS = 1e-6
NEG = -1e30
PAD_W = 2 * GRID_W - 1
BW = 7 * P
IW = 5 * P


def key_tiles(t):
    if t < 2:
        return 0, 4
    if t > 5:
        return 4, 4
    return t - 2, 5


def constants():
    tok = np.arange(S)
    inv = (1.0 / (10000.0 ** (np.arange(0, 32, 2, dtype=np.float32) / np.float32(32)))).astype(np.float32)
    row, col = (tok // GRID_W).astype(np.float32), (tok % GRID_W).astype(np.float32)
    ang = np.concatenate([row[:, None] * inv[None], col[:, None] * inv[None]], -1)
    cos, sin = np.cos(ang), np.sin(ang)
    cc = np.repeat(cos, 2, -1)
    ss = np.stack([-sin, sin], -1).reshape(S, HD)
    rope = np.stack([cc, ss]).astype(np.float32)
    c = np.arange(GRID_W)
    start = np.clip(c - 8, 0, GRID_W - 16)
    ok = (c[None, :] >= start[:, None]) & (c[None, :] < start[:, None] + 16)
    qr = np.arange(2)
    rr = np.arange(-6, 8)
    wide = np.broadcast_to(ok[None, :, None, :], (2, 64, 14, 64))
    dr = rr[None, :] - qr[:, None]
    rows_ok = ((dr >= -4) & (dr <= 3))[:, None, :, None]
    inner = (wide & rows_ok)[:, :, 2:12]
    mask = np.concatenate([wide.reshape(P, BW), inner.reshape(P, IW)], -1)
    return {
        "ident": np.eye(P, dtype=np.float32),
        "rope": rope,
        "mask": np.where(mask, 0.0, NEG).astype(np.float32),
    }


class Chain:

    def __init__(self, eng, sem, base=0):
        self.eng, self.sem, self.base, self.n = eng, sem, base, 0

    def link(self, ins):
        self.n += 1
        ins.then_inc(self.sem, 1)
        self.eng.wait_ge(self.sem, self.base + self.n)


def project(nc, d, keep):
    proj, ident = keep["proj"], keep["ident"]
    with ExitStack() as ctx:
        sb = lambda name, shape, dt=F32: ctx.enter_context(nc.sbuf_tensor(name, shape, dt))
        ps = lambda name, shape: ctx.enter_context(nc.psum_tensor(name, shape, F32))
        sem = lambda name: ctx.enter_context(nc.semaphore(name))
        xt = sb("p_x", [P, 2, D])
        sq = sb("p_sq", [P, D])
        ss = sb("p_ss", [P, NT])
        ms = sb("p_ms", [P, NT])
        rstd = sb("p_rstd", [P, NT])
        pw = sb("p_pow", [P, NT])
        g1 = sb("p_g1", [P, KD])
        xh = sb("p_xh", [P, KD, S], F32R)
        xl = sb("p_xl", [P, KD, S], F32R)
        w32 = sb("p_w32", [P, 2, KD, GW])
        wh = sb("p_wh", [P, 2, KD, GW], F32R)
        wl = sb("p_wl", [P, 2, KD, GW], F32R)
        tp = [ps(f"p_tp{b}", [P, 512]) for b in range(4)]
        acc = [ps(f"p_acc{b}", [P, 512]) for b in range(4)]
        x_in = [sem(f"p_x_in{b}") for b in range(2)]
        small_in = sem("p_small_in")
        w_in = [sem(f"p_w_in{b}") for b in range(2)]
        squared, rows_out = sem("p_squared"), sem("p_rows_out")
        means = sem("p_means")
        powc = sem("p_powc")
        rstd_ok = sem("p_rstd_ok")
        turned = sem("p_turned")
        x_hi, x_lo = sem("p_x_hi"), sem("p_x_lo")
        w_hi, w_lo = sem("p_w_hi"), sem("p_w_lo")
        group_done = sem("p_group_done")
        acc_full = sem("p_acc_full")
        acc_act, acc_dve = sem("p_acc_act"), sem("p_acc_dve")
        block = ctx.enter_context(nc.Block())

        w_src = d["w_in"][0].rearrange("(k p) n -> p k n", p=P)

        @block.sync
        def _(sp):
            sp.dma_start(ident[:], d["ident"]).then_inc(small_in, 16)
            with nc.allow_non_contiguous_dma(reason="a gain vector by partition, once"):
                sp.dma_start(g1[:], d["norm1_g"][0].rearrange("(k p) -> p k", p=P)).then_inc(small_in, 16)
            for t in range(NT):
                if t >= 2:
                    sp.wait_ge(squared, t - 1)
                    sp.wait_ge(turned, 2 * (t - 1))
                sp.dma_start(xt[:, t % 2, :], d["x"][0, t * P:(t + 1) * P, :]).then_inc(x_in[t % 2], 16)
            for h in range(NH):
                sp.dma_start(d["rows"][h], d["rpb"][h].unsqueeze(1).to_broadcast([15, GRID_W, PAD_W])).then_inc(rows_out, 16)
            for n in range(NG):
                if n >= 2:
                    sp.wait_ge(w_lo, n - 1)
                sp.dma_start(w32[:, n % 2], w_src[:, :, n * GW:(n + 1) * GW]).then_inc(w_in[n % 2], 16)
            sp.wait_ge(rows_out, 16 * NH)

        @block.gpsimd
        def _(pool):
            nc.gpsimd.memset(pw[:], -0.5).then_inc(powc, 1)
            pool.wait_ge(powc, 1)
            pool.wait_ge(means, 1)
            nc.gpsimd.tensor_tensor(rstd[:], ms[:], pw[:], ALU.pow).then_inc(rstd_ok, 1)

        @block.scalar
        def _(act):
            for t in range(NT):
                act.wait_ge(x_in[t % 2], 16 * (t // 2 + 1))
                if t:
                    act.wait_ge(squared, t)
                nc.scalar.activation(sq[:], xt[:, t % 2, :], ACT.Square, accum_out=ss[:, t:t + 1]).then_inc(squared, 1)
                for h in range(2):
                    act.wait_ge(turned, 2 * t + h + 1)
                    nc.scalar.copy(xh[:, 4 * h:4 * h + 4, t * P:(t + 1) * P],
                                   tp[(2 * t + h) % 4][:].rearrange("p (k c) -> p k c", k=4)).then_inc(x_hi, 1)

            def split_hi(n):
                act.wait_ge(w_in[n % 2], 16 * (n // 2 + 1))
                if n >= 2:
                    act.wait_ge(group_done, n - 1)
                for k in range(KD):
                    ins = nc.scalar.activation(wh[:, n % 2, k, :], w32[:, n % 2, k, :], ACT.Copy, scale=g1[:, k:k + 1])
                ins.then_inc(w_hi, 1)

            act.wait_ge(small_in, 32)
            split_hi(0)
            split_hi(1)
            act.wait_ge(rstd_ok, 1)
            for n in range(NG):
                for t in range(0, NT, 2):
                    act.wait_ge(acc_full, n * NT + t + 1)
                    nc.scalar.activation(proj[:, t, n * GW:(n + 1) * GW], acc[t % 4][:, 0:GW], ACT.Copy,
                                         scale=rstd[:, t:t + 1]).then_inc(acc_act, 1)
                if n + 2 < NG:
                    split_hi(n + 2)
            act.wait_ge(acc_act, NG * NT // 2)

        @block.vector
        def _(dve):
            for t in range(NT):
                for h in range(2):
                    dve.wait_ge(x_hi, 2 * t + h + 1)
                    cols = (slice(None), slice(4 * h, 4 * h + 4), slice(t * P, (t + 1) * P))
                    nc.vector.tensor_tensor(xl[cols], tp[(2 * t + h) % 4][:].rearrange("p (k c) -> p k c", k=4),
                                            xh[cols].bitcast(F32), ALU.subtract).then_inc(x_lo, 1)
            dve.wait_ge(squared, NT)
            nc.vector.tensor_scalar(ms[:], ss[:], 1.0 / D, EPS, ALU.mult, ALU.add).then_inc(means, 1)

            def split_lo(n):
                dve.wait_ge(w_hi, n + 1)
                for k in range(KD):
                    ins = nc.vector.scalar_tensor_tensor(out=wl[:, n % 2, k, :], in0=w32[:, n % 2, k, :], scalar=g1[:, k:k + 1],
                                                         in1=wh[:, n % 2, k, :].bitcast(F32), op0=ALU.mult, op1=ALU.subtract)
                ins.then_inc(w_lo, 1)

            dve.wait_ge(small_in, 32)
            split_lo(0)
            split_lo(1)
            dve.wait_ge(rstd_ok, 1)
            for n in range(NG):
                for t in range(1, NT, 2):
                    dve.wait_ge(acc_full, n * NT + t + 1)
                    nc.vector.tensor_scalar(proj[:, t, n * GW:(n + 1) * GW], acc[t % 4][:, 0:GW], rstd[:, t:t + 1],
                                            None, ALU.mult).then_inc(acc_dve, 1)
                if n + 2 < NG:
                    split_lo(n + 2)
            dve.wait_ge(acc_dve, NG * NT // 2)

        @block.tensor
        def _(pe):
            pe.wait_ge(small_in, 32)
            for t in range(NT):
                pe.wait_ge(x_in[t % 2], 16 * (t // 2 + 1))
                for h in range(2):
                    if 2 * t + h >= 4:
                        pe.wait_ge(x_lo, 2 * t + h - 3)
                    for k in range(4):
                        ins = nc.tensor.transpose(tp[(2 * t + h) % 4][:, k * P:(k + 1) * P],
                                                  xt[:, t % 2, (4 * h + k) * P:(4 * h + k + 1) * P], ident[:])
                    ins.then_inc(turned, 1)

            def group(n, b, first):
                pe.wait_ge(w_lo, n + 1)
                for t in range(NT):
                    if first and t >= 4:
                        pe.wait_ge(acc_dve if t % 2 else acc_act, t // 2 - 1)
                    elif not first:
                        pe.wait_ge(acc_dve if t % 2 else acc_act, 4 * n + t // 2 - 1)
                    cols = slice(t * P, (t + 1) * P)
                    for k in range(KD):
                        for m, (x, w) in enumerate(((xh, wh), (xh, wl), (xl, wh))):
                            ins = nc.tensor.matmul(acc[t % 4][:, 0:GW], x[:, k, cols], w[:, b, k, :],
                                                   start=(k == 0 and m == 0), stop=(k == KD - 1 and m == 2))
                    ins.then_inc(acc_full, 1)
                pe.wait_ge(acc_full, (n + 1) * NT)
                pe.sem_inc(group_done, 1)

            pe.wait_ge(x_lo, 2 * NT)
            group(0, 0, True)
            with pe.Fori(0, (NG - 1) // 2) as i:
                group(2 * i + 1, 1, False)
                group(2 * i + 2, 0, False)


def attend(nc, d, keep):
    proj, ident = keep["proj"], keep["ident"]
    with ExitStack() as ctx:
        sb = lambda name, shape, dt=F32: ctx.enter_context(nc.sbuf_tensor(name, shape, dt))
        ps = lambda name, shape: ctx.enter_context(nc.psum_tensor(name, shape, F32))
        sem = lambda name: ctx.enter_context(nc.semaphore(name))
        gains = sb("a_gains", [P, 4, HD])
        rope = sb("a_rope", [P, 2, NT, HD])
        mask = sb("a_mask", [P, BW + IW])
        raw = sb("a_raw", [P, 2, 14, GRID_W])
        bias = sb("a_bias", [P, 2, BW + IW])
        sq = sb("a_sq", [P, NT, P])
        ssq = sb("a_ssq", [P, 2, NT, 2])
        rs = sb("a_rs", [P, 2, NT, 2])
        pw = sb("a_pow", [P, 2 * NT])
        qk = sb("a_qk", [P, 2, NT, P])
        swp = sb("a_swp", [P, NT, P])
        q1 = [sb(f"a_q1{b}", [P, S], F32R) for b in range(2)]
        k1 = [sb(f"a_k1{b}", [P, S], F32R) for b in range(2)]
        k2 = [sb(f"a_k2{b}", [HD, S], F32R) for b in range(2)]
        negs = sb("a_negs", [P, 2, IW])
        negm = sb("a_negm", [P, 2, NT])
        rsum = sb("a_rsum", [P, 2, NT])
        rinv = sb("a_rinv", [P, NT])
        prob = sb("a_prob", [P, 2, S])
        probT = [sb(f"a_probT{b}", [P, S]) for b in range(2)]
        spsum = [ps(f"a_s{b}", [P, 2, 512]) for b in range(2)]
        turn = [ps(f"a_turn{b}", [P, 512]) for b in range(2)]
        opsum = [ps(f"a_o{b}", [P, NT, HD]) for b in range(2)]
        gain_in, rope_in = sem("a_gain_in"), sem("a_rope_in")
        raw_in = [sem(f"a_raw_in{b}") for b in range(2)]
        bias_ok, setup = sem("a_bias_ok"), sem("a_setup")
        pool_own, dve_own = sem("a_pool_own"), sem("a_dve_own")
        squared, reduced, ready, loaded = sem("a_squared"), sem("a_reduced"), sem("a_ready"), sem("a_loaded")
        hi_ok, passed = sem("a_hi_ok"), sem("a_passed")
        full = [sem(f"a_full{b}") for b in range(2)]
        free = [sem(f"a_free{b}") for b in range(2)]
        scored, maxed, exped, summed, o_free = sem("a_scored"), sem("a_maxed"), sem("a_exped"), sem("a_summed"), sem("a_o_free")
        block = ctx.enter_context(nc.Block())
        NA, GQ = 0, 1
        per_head = {NA: (NT + 1, sum(key_tiles(t)[1] > 4 for t in range(NT)) + 1), GQ: (NT + 1, NT + 1)}
        TURN_AT = {2: 0, 4: 1}

        def tiles(kind, t):
            return (0, NT) if kind == GQ else key_tiles(t)

        def uses_before(kind, h, b):
            return 1 + (per_head[NA][b] * h if kind == NA else per_head[NA][b] * NH + per_head[GQ][b] * h)

        def use(kind, h, b, t, turning=False):
            n = 0
            for s in range(t + 1):
                n += 1 if b == 0 or tiles(kind, s)[1] > 4 else 0
                if TURN_AT.get(s) == b and (s < t or turning) and not (kind == GQ and isinstance(h, int) and h == NH - 1):
                    n += 1
            return uses_before(kind, h, b) + n

        def heads(eng, body):
            for kind in (NA, GQ):
                with eng.Fori(0, NH // 2 - 1) as i:
                    for b in range(2):
                        body(kind, 2 * i + b, b, kind)
                body(kind, NH - 2, 0, kind)
                body(kind, NH - 1, 1, GQ if kind == NA else None)

        def step_of(kind, h, t):
            return (h + NH * kind) * NT + t

        @block.sync
        def _(sp):
            for n, name in enumerate(("na_q_norm_g", "na_k_norm_g", "gqa_q_norm_g", "gqa_k_norm_g")):
                sp.dma_start(gains[:, n, :], d[name].to_broadcast([P, HD])).then_inc(gain_in, 16)
            sp.dma_start(mask[:], d["mask"]).then_inc(gain_in, 16)
            for n in range(2):
                sp.dma_start(rope[:, n], d["rope"][n].rearrange("(t p) c -> p t c", p=P)).then_inc(rope_in, 16)
            for h in range(NH):
                if h >= 2:
                    sp.wait_ge(bias_ok, h - 1)
                for qr in range(2):
                    t = d["rows"]
                    src = bass.AP(t.tensor, t.offset + (h * 15 + 1 - qr) * GRID_W * PAD_W + GRID_W - 1,
                                  [[PAD_W - 1, GRID_W], [GRID_W * PAD_W, 14], [1, GRID_W]])
                    sp.dma_start(raw[qr * GRID_W:(qr + 1) * GRID_W, h % 2], src).then_inc(raw_in[h % 2], 16)

        @block.gpsimd
        def _(pool):
            nc.gpsimd.memset(pw[:], -0.5).then_inc(setup, 1)
            pool.wait_ge(gain_in, 80)
            for n in (0, 2):
                ins = nc.gpsimd.tensor_scalar(gains[:, n, :], gains[:, n, :], HD ** -0.5, None, ALU.mult)
            ins.then_inc(setup, 1)
            pool.wait_ge(setup, 2)
            pool.wait_ge(rope_in, 32)
            LINKS = (4, 5)

            def prepare(kind, h, b, first=False):
                j = h + NH * kind
                own = Chain(pool, pool_own, LINKS[NA] * h if kind == NA else LINKS[NA] * NH + LINKS[GQ] * h)
                if kind == NA:
                    qc = proj[:, :, bass.ds(NQ0 + h * HD, HD)]
                    kc = proj[:, :, bass.ds(NK0 + h * HD, HD)]
                else:
                    qc = proj[:, :, bass.ds(GQ0 + h * HD, HD)]
                    kv = kv_of(h)
                    kc = proj[:, :, bass.ds(GK0 + kv * HD, HD)]
                dst = qk[:, b]
                pool.sem_inc(passed, 1)
                nc.gpsimd.tensor_tensor(sq[:, :, 0:HD], qc, qc, ALU.mult)
                nc.gpsimd.tensor_tensor(sq[:, :, HD:P], kc, kc, ALU.mult).then_inc(squared, 1)
                pool.wait_ge(reduced, j + 1)
                own.link(nc.gpsimd.tensor_tensor(rs[:, b].rearrange("p t w -> p (t w)"),
                                                 ssq[:, b].rearrange("p t w -> p (t w)"), pw[:], ALU.pow))
                if not first:
                    pool.wait_ge(loaded, j - 1)
                    pool.sem_inc(passed, 1)
                for w, c in enumerate((qc, kc)):
                    ins = nc.gpsimd.tensor_tensor(dst[:, :, w * HD:(w + 1) * HD], c,
                                                  rs[:, b, :, w:w + 1].to_broadcast([P, NT, HD]), ALU.mult)
                own.link(ins)
                for w in range(2):
                    part = dst[:, :, w * HD:(w + 1) * HD]
                    ins = nc.gpsimd.tensor_tensor(part, part, gains[:, 2 * kind + w, :].unsqueeze(1).to_broadcast([P, NT, HD]), ALU.mult)
                if kind == NA:
                    own.link(ins)
                    pool.sem_inc(ready, 1)
                    pool.wait_ge(raw_in[b], 32 * (h // 2 + 1) if first else 32 * (half_of(h, b) + 1))
                    if not first:
                        pool.wait_ge(maxed, (h - 1) * NT + 1)
                    flat = raw[:, b].rearrange("p r c -> p (r c)")
                    nc.gpsimd.tensor_tensor(bias[:, b, 0:BW], flat, mask[:, 0:BW], ALU.add)
                    own.link(nc.gpsimd.tensor_tensor(bias[:, b, BW:], flat[:, P:P + IW], mask[:, BW:], ALU.add))
                    pool.sem_inc(bias_ok, 1)
                    return
                own.link(ins)
                pairs = dst.rearrange("p t (w c two) -> p t w c two", w=2, two=2)
                sw = swp[:].rearrange("p t (w c two) -> p t w c two", w=2, two=2)
                sn = rope[:, 1].rearrange("p t (c two) -> p t c two", two=2)
                for w in range(2):
                    for o in range(2):
                        ins = nc.gpsimd.tensor_tensor(sw[:, :, w, :, o], pairs[:, :, w, :, 1 - o], sn[:, :, :, o], ALU.mult)
                own.link(ins)
                for w in range(2):
                    part = dst[:, :, w * HD:(w + 1) * HD]
                    ins = nc.gpsimd.tensor_tensor(part, part, rope[:, 0], ALU.mult)
                own.link(ins)
                nc.gpsimd.tensor_tensor(dst, dst, swp[:], ALU.add).then_inc(ready, 1)

            def kv_of(h):
                return kv_now[0]

            def half_of(h, b):
                return now[0]

            kv_now, now = [0], [0]
            prepare(NA, 0, 0, True)
            prepare(NA, 1, 1, True)
            with pool.Fori(1, NH // 2) as i:
                now[0] = i
                for b in range(2):
                    prepare(NA, 2 * i + b, b)
            for kv in range(KVH):
                kv_now[0] = kv
                with pool.Fori(2 * kv, 2 * kv + 2) as i:
                    for b in range(2):
                        prepare(GQ, 2 * i + b, b)

        @block.tensor
        def _(pe):
            def load(b, piece, n_free):
                if n_free is not None:
                    pe.wait_ge(free[piece], n_free)
                for c in range(4):
                    ins = nc.tensor.transpose(turn[piece][:, c * P:(c + 1) * P], qk[:, b, 4 * piece + c, :], ident[:])
                ins.then_inc(full[piece], 1)

            def score(kind, h, b, t):
                g = step_of(kind, h, t)
                k0, n = tiles(kind, t)
                if not (kind == NA and isinstance(h, int) and h == 0 and t < 2):
                    pe.wait_ge(exped if kind == GQ else maxed, g)
                w = 4 * P if n != 5 else IW // 2
                for half in range(1 if n == 4 else 2):
                    cols = slice(k0 * P + half * w, k0 * P + (half + 1) * w)
                    out = spsum[t % 2][:, half, 0:w]
                    q = slice(t * P, (t + 1) * P)
                    nc.tensor.matmul(out, q1[b][:, q], k1[b][:, cols], start=True, stop=False)
                    ins = nc.tensor.matmul(out, q1[b][0:HD, q], k2[b][:, cols], start=False, stop=True)
                ins.then_inc(scored, 1)

            def turn_probs(kind, h, t):
                pe.wait_ge(exped, step_of(kind, h, t) + 2)
                k0, n = tiles(kind, t)
                for bank in range(2 if n > 4 else 1):
                    pe.wait_ge(free[bank], use(kind, h, bank, t) - 1)
                    for c in range(4 * bank, min(n, 4 * bank + 4)):
                        ins = nc.tensor.transpose(turn[bank][:, (c % 4) * P:(c % 4 + 1) * P],
                                                  prob[:, t % 2, c * P:(c + 1) * P], ident[:])
                    ins.then_inc(full[bank], 1)

            def weigh(kind, h, b, t):
                k0, n = tiles(kind, t)
                if t == 0:
                    pe.wait_ge(o_free, h + NH * kind + 1)
                for bank in range(2 if n > 4 else 1):
                    pe.wait_ge(free[bank], use(kind, h, bank, t))
                for c in range(n):
                    v = NV0 + h * HD if kind == NA else GV0 + kv_now[0] * HD
                    ins = nc.tensor.matmul(opsum[b][:, t, :], probT[t % 2][:, c * P:(c + 1) * P],
                                           proj[:, k0 + c, bass.ds(v, HD)], start=(c == 0), stop=(c == n - 1))
                ins.then_inc(summed, 1)

            def head(kind, h, b, nxt):
                for t in range(NT):
                    if t + 1 < NT:
                        score(kind, h, b, t + 1)
                    elif nxt is not None:
                        for piece in range(2):
                            at = [s for s in TURN_AT if TURN_AT[s] == piece][0]
                            pe.wait_ge(free[piece], use(kind, h, piece, at, True))
                        score(nxt, 0 if nxt != kind else h + 1, 1 - b, 0)
                    turn_probs(kind, h, t)
                    if t in TURN_AT and nxt is not None:
                        load(1 - b, TURN_AT[t], use(kind, h, TURN_AT[t], t))
                        if TURN_AT[t] == 1:
                            pe.wait_ge(full[1], use(kind, h, 1, t, True))
                            pe.sem_inc(loaded, 1)
                    if t == 0 and nxt is not None:
                        pe.wait_ge(ready, h + NH * kind + 2)
                    if t:
                        weigh(kind, h, b, t - 1)
                weigh(kind, h, b, NT - 1)

            kv_now = [0]
            pe.sem_inc(summed, 1)
            pe.wait_ge(ready, 1)
            for piece in range(2):
                load(0, piece, None)
            pe.wait_ge(full[1], 1)
            pe.sem_inc(loaded, 1)
            for piece in range(2):
                pe.wait_ge(free[piece], 1)
            score(NA, 0, 0, 0)
            with pe.Fori(0, NH // 2 - 1) as i:
                for b in range(2):
                    head(NA, 2 * i + b, b, NA)
            head(NA, NH - 2, 0, NA)
            head(NA, NH - 1, 1, GQ)
            with pe.Fori(0, 2) as i:
                for b in range(2):
                    head(GQ, 2 * i + b, b, GQ)
            kv_now[0] = 1
            head(GQ, 4, 0, GQ)
            head(GQ, 5, 1, GQ)
            head(GQ, 6, 0, GQ)
            head(GQ, 7, 1, None)

        @block.scalar
        def _(act):
            def split_hi(b, piece, n_full):
                act.wait_ge(full[piece], n_full)
                c = slice(piece * 512, (piece + 1) * 512)
                nc.scalar.copy(q1[b][0:HD, c], turn[piece][0:HD, :])
                nc.scalar.copy(k1[b][0:HD, c], turn[piece][HD:P, :])
                nc.scalar.copy(k1[b][HD:P, c], turn[piece][HD:P, :]).then_inc(hi_ok, 1)

            def exponent(kind, h, b, t):
                g = step_of(kind, h, t)
                act.wait_ge(maxed, g + 2)
                k0, n = tiles(kind, t)
                out = prob[:, t % 2, 0:n * P]
                t2 = (t - 2) % NT
                if tiles(kind, t2)[1] > 4 and t >= 2:
                    act.wait_ge(full[1], use(kind, h, 1, t2))
                elif t < 2 and kind == GQ:
                    act.wait_ge(full[1], uses_before(kind, h, 1))
                if kind == NA:
                    ins = nc.scalar.activation(out, negs[:, t % 2, 0:n * P], ACT.Exp, bias=negm[:, b, t:t + 1], scale=-1.0,
                                               accum_out=rsum[:, b, t:t + 1])
                else:
                    ins = nc.scalar.activation(out.rearrange("p (h c) -> p h c", h=2), spsum[t % 2][:], ACT.Exp,
                                               bias=negm[:, b, t:t + 1], accum_out=rsum[:, b, t:t + 1])
                ins.then_inc(exped, 1)

            def head(kind, h, b, nxt):
                for t in range(NT):
                    k0, n = tiles(kind, t)
                    act.wait_ge(full[0], use(kind, h, 0, t))
                    g = step_of(kind, h, t)
                    act.wait_ge(summed, g if t else g + 1)
                    nc.scalar.copy(probT[t % 2][:, 0:4 * P], turn[0][:]).then_inc(free[0], 1)
                    if t in TURN_AT and nxt is not None:
                        split_hi(1 - b, TURN_AT[t], use(kind, h, TURN_AT[t], t, True))
                    if t + 1 < NT:
                        exponent(kind, h, b, t + 1)
                    elif nxt is not None:
                        exponent(nxt, 0 if nxt != kind else h + 1, 1 - b, 0)

            act.sem_inc(exped, 1)
            for piece in range(2):
                split_hi(0, piece, 1)
            exponent(NA, 0, 0, 0)
            heads(act, head)

        @block.vector
        def _(dve):
            dve.sem_inc(o_free, 2)
            dve.sem_inc(maxed, 1)
            nc_reduce = nc.vector.tensor_reduce

            def sums(j, b):
                dve.wait_ge(squared, j + 1)
                own.link(nc_reduce(ssq[:, b].rearrange("p t w -> p (t w)"), sq[:].rearrange("p t (w c) -> p (t w) c", w=2), AX, ALU.add))
                flat = ssq[:, b].rearrange("p t w -> p (t w)")
                nc.vector.tensor_scalar(flat, flat, 1.0 / HD, EPS, ALU.mult, ALU.add).then_inc(reduced, 1)

            def split_lo(b, piece):
                c = slice(piece * 512, (piece + 1) * 512)
                nc.vector.tensor_tensor(q1[b][HD:P, c], turn[piece][0:HD, :], q1[b][0:HD, c].bitcast(F32), ALU.subtract)
                nc.vector.tensor_tensor(k2[b][:, c], turn[piece][HD:P, :], k1[b][HD:P, c].bitcast(F32),
                                        ALU.subtract).then_inc(free[piece], 1)

            def maxima(kind, h, b, t):
                g = step_of(kind, h, t)
                dve.wait_ge(scored, g + 1)
                k0, n = tiles(kind, t)
                m = negm[:, b, t:t + 1]
                if kind == GQ:
                    nc_reduce(m, spsum[t % 2][:].rearrange("p h c -> p (h c)"), AX, ALU.max, negate=True).then_inc(maxed, 1)
                    return
                if not (isinstance(h, int) and h == 0 and t < 2):
                    dve.wait_ge(exped, g)
                if t == 0:
                    dve.wait_ge(bias_ok, h + 1)
                if n == 4:
                    o = (k0 - t + 3) * P
                    s, bb, out = spsum[t % 2][:, 0, :], bias[:, b, o:o + 4 * P], negs[:, t % 2, 0:4 * P]
                else:
                    s, bb, out = (spsum[t % 2][:, :, 0:IW // 2], bias[:, b, BW:].rearrange("p (h c) -> p h c", h=2),
                                  negs[:, t % 2, :].rearrange("p (h c) -> p h c", h=2))
                dve.sem_inc(passed, 1)
                nc.vector.tensor_tensor_reduce(out=out, in0=s, in1=bb, scale=-1.0, scalar=3.0e38, op0=ALU.add,
                                               op1=ALU.min, accum_out=m).then_inc(maxed, 1)

            def head(kind, h, b, nxt):
                j = h + NH * kind
                own.base, own.n = 2 + 2 * j, 0
                for t in range(NT):
                    if t + 1 < NT:
                        maxima(kind, h, b, t + 1)
                    elif nxt is not None:
                        maxima(nxt, 0 if nxt != kind else h + 1, 1 - b, 0)
                    k0, n = tiles(kind, t)
                    if n > 4:
                        dve.wait_ge(full[1], use(kind, h, 1, t))
                        g = step_of(kind, h, t)
                        dve.wait_ge(summed, g if t else g + 1)
                        nc.vector.tensor_copy(probT[t % 2][:, 4 * P:n * P], turn[1][:, 0:(n - 4) * P]).then_inc(free[1], 1)
                    if t in TURN_AT and nxt is not None:
                        dve.wait_ge(hi_ok, 2 * j + 3 + TURN_AT[t])
                        split_lo(1 - b, TURN_AT[t])
                    if t == 1 and not (kind == GQ and isinstance(h, int) and h >= NH - 2):
                        sums(j + 2, b)
                    elif t == 1:
                        own.link(nc.vector.memset(rinv[:], 1.0))
                dve.wait_ge(summed, (j + 1) * NT + 1)
                own.link(nc.vector.reciprocal(rinv[:], rsum[:, b, :]))
                c0 = (GQ0 if kind == GQ else NQ0) + h * HD
                nc.vector.tensor_tensor(proj[:, :, bass.ds(c0, HD)], opsum[b][:], rinv[:].unsqueeze(2).to_broadcast([P, NT, HD]),
                                        ALU.mult).then_inc(o_free, 1)

            own = Chain(dve, dve_own)
            sums(0, 0)
            sums(1, 1)
            for piece in range(2):
                dve.wait_ge(hi_ok, piece + 1)
                split_lo(0, piece)
            maxima(NA, 0, 0, 0)
            heads(dve, head)
            dve.wait_ge(o_free, 2 * NH + 2)


def mix(nc, d, keep):
    proj, ident, affT = keep["proj"], keep["ident"], keep["affT"]
    with ExitStack() as ctx:
        sb = lambda name, shape, dt=F32: ctx.enter_context(nc.sbuf_tensor(name, shape, dt))
        ps = lambda name, shape: ctx.enter_context(nc.psum_tensor(name, shape, F32))
        sem = lambda name: ctx.enter_context(nc.semaphore(name))
        wo32 = sb("m_wo32", [P, 2, D])
        woh, wol = sb("m_woh", [P, KD, D], F32R), sb("m_wol", [P, KD, D], F32R)
        go = sb("m_go", [P, KD])
        g2 = sb("m_g2", [P, D])
        wr = sb("m_wr", [P, KD, E])
        pw = sb("m_pow", [P, 2])
        xt = sb("m_x", [P, 2, D])
        sq = sb("m_sq", [P, D])
        ss, ms, rs = sb("m_ss", [P, NT, 2]), sb("m_ms", [P, NT, 2]), sb("m_rs", [P, NT, 2])
        ss2, ms2, rs2 = sb("m_ss2", [P, NT]), sb("m_ms2", [P, NT]), sb("m_rs2", [P, NT])
        mx = sb("m_mix", [P, D])
        mh = [sb(f"m_mh{b}", [P, KD, P], F32R) for b in range(2)]
        ml = [sb(f"m_ml{b}", [P, KD, P], F32R) for b in range(2)]
        x1 = sb("m_x1", [P, 2, D])
        hn = sb("m_hn", [P, 2, D])
        hT = sb("m_hT", [P, KD, P])
        nmax, den, rden = sb("m_nmax", [P, NT]), sb("m_den", [P, NT]), sb("m_rden", [P, NT])
        ex, aff = sb("m_ex", [P, E]), sb("m_aff", [P, E])
        ta = [ps(f"m_ta{b}", [P, 512]) for b in range(2)]
        tc = [ps(f"m_tc{b}", [P, 512]) for b in range(2)]
        acc = ps("m_acc", [P, 2, 512])
        lg, at = ps("m_lg", [P, 512]), ps("m_at", [P, 512])
        small_in, powc = sem("m_small_in"), sem("m_powc")
        wo_in = [sem(f"m_wo_in{b}") for b in range(2)]
        x_in = [sem(f"m_x_in{b}") for b in range(2)]
        stored = [sem(f"m_stored{b}") for b in range(2)]
        wo_hi, wo_lo = sem("m_wo_hi"), sem("m_wo_lo")
        sq_a, ms_a, rs_a, mixed, turned_a, hi_a, lo_a = (sem(f"m_{n}") for n in ("sq_a", "ms_a", "rs_a", "mixed", "turned_a", "hi_a", "lo_a"))
        multiplied, x1_ok, sq_c, ms_c, rs_c, hn_ok, turned_c, copied_c = (
            sem(f"m_{n}") for n in ("multiplied", "x1_ok", "sq_c", "ms_c", "rs_c", "hn_ok", "turned_c", "copied_c"))
        logits, maxed, exped, recip, aff_ok, aff_turned, affT_ok = (
            sem(f"m_{n}") for n in ("logits", "maxed", "exped", "recip", "aff_ok", "aff_turned", "affT_ok"))
        block = ctx.enter_context(nc.Block())
        half = lambda h: slice(512 * h, 512 * h + 512)

        @block.sync
        def _(sp):
            with nc.allow_non_contiguous_dma(reason="gain vectors by partition, once"):
                sp.dma_start(go[:, 0:4], d["na_out_g"][0].rearrange("(k p) -> p k", p=P)).then_inc(small_in, 16)
                sp.dma_start(go[:, 4:8], d["gqa_out_g"][0].rearrange("(k p) -> p k", p=P)).then_inc(small_in, 16)
            sp.dma_start(g2[:], d["norm2_g"].to_broadcast([P, D])).then_inc(small_in, 16)
            sp.dma_start(wr[:], d["w_router"][0].rearrange("(k p) e -> p k e", p=P)).then_inc(small_in, 16)
            for k in range(KD):
                if k >= 2:
                    sp.wait_ge(wo_lo, k - 1)
                sp.dma_start(wo32[:, k % 2, :], d["w_out"][0, k * P:(k + 1) * P, :]).then_inc(wo_in[k % 2], 16)
            for t in range(NT + 1):
                if t < NT:
                    if t >= 2:
                        sp.wait_ge(x1_ok, t - 1)
                    sp.dma_start(xt[:, t % 2, :], d["x"][0, t * P:(t + 1) * P, :]).then_inc(x_in[t % 2], 16)
                if t:
                    u = t - 1
                    sp.wait_ge(x1_ok, u + 1)
                    sp.dma_start(d["out"][u * P:(u + 1) * P, :], x1[:, u % 2, :]).then_inc(stored[u % 2], 16)
                    sp.wait_ge(hn_ok, u + 1)
                    sp.dma_start(d["hn"][u * P:(u + 1) * P, :], hn[:, u % 2, :]).then_inc(stored[u % 2], 16)
            for b in range(2):
                sp.wait_ge(stored[b], 32 * NT // 2)

        @block.gpsimd
        def _(pool):
            nc.gpsimd.memset(pw[:], -0.5).then_inc(powc, 1)
            pool.wait_ge(powc, 1)
            for t in range(-1, NT + 2):
                if t + 1 < NT:
                    pool.wait_ge(ms_a, t + 2)
                    nc.gpsimd.tensor_tensor(rs[:, t + 1, :], ms[:, t + 1, :], pw[:], ALU.pow).then_inc(rs_a, 1)
                if t >= 2:
                    pool.wait_ge(ms_c, t - 1)
                    nc.gpsimd.tensor_tensor(rs2[:, t - 2:t - 1], ms2[:, t - 2:t - 1], pw[:, 0:1], ALU.pow).then_inc(rs_c, 1)

        @block.scalar
        def _(act):
            act.wait_ge(small_in, 64)

            def squares(t):
                if t:
                    act.wait_ge(sq_a, 2 * t)
                nc.scalar.activation(sq[:, 0:512], proj[:, t, NQ0:NQ0 + 512], ACT.Square, accum_out=ss[:, t, 0:1]).then_inc(sq_a, 1)
                nc.scalar.activation(sq[:, 512:1024], proj[:, t, GQ0:GQ0 + 512], ACT.Square, accum_out=ss[:, t, 1:2]).then_inc(sq_a, 1)

            def stage_a(t):
                for h in range(2):
                    act.wait_ge(turned_a, 2 * t + h + 1)
                    nc.scalar.copy(mh[t % 2][:, 4 * h:4 * h + 4, :], ta[h][:].rearrange("p (k c) -> p k c", k=4)).then_inc(hi_a, 1)

            def stage_c(t):
                act.wait_ge(x1_ok, t + 1)
                nc.scalar.activation(hn[:, t % 2, :], x1[:, t % 2, :], ACT.Square, accum_out=ss2[:, t:t + 1]).then_inc(sq_c, 1)
                for h in range(2):
                    act.wait_ge(turned_c, 2 * t + h + 1)
                    nc.scalar.copy(hT[:, 4 * h:4 * h + 4, :], tc[h][:].rearrange("p (k c) -> p k c", k=4)).then_inc(copied_c, 1)
                act.wait_ge(maxed, t + 1)
                nc.scalar.activation(ex[:], lg[:, 0:E], ACT.Exp, bias=nmax[:, t:t + 1], accum_out=den[:, t:t + 1]).then_inc(exped, 1)

            for k in range(KD):
                act.wait_ge(wo_in[k % 2], 16 * (k // 2 + 1))
                nc.scalar.activation(woh[:, k, :], wo32[:, k % 2, :], ACT.Copy, scale=go[:, k:k + 1]).then_inc(wo_hi, 1)
                if k == 0:
                    squares(0)
            for t in range(NT + 2):
                if t + 1 < NT:
                    squares(t + 1)
                if t < NT:
                    stage_a(t)
                if t >= 2:
                    stage_c(t - 2)

        @block.vector
        def _(dve):
            dve.wait_ge(small_in, 64)

            def normalise(t):
                dve.wait_ge(sq_a, 2 * t + 2)
                nc.vector.tensor_scalar(ms[:, t, :], ss[:, t, :], 1.0 / 512, EPS, ALU.mult, ALU.add).then_inc(ms_a, 1)
                dve.wait_ge(rs_a, t + 1)
                if t:
                    dve.wait_ge(turned_a, 2 * t)
                for h, c0 in enumerate((NQ0, GQ0)):
                    ins = nc.vector.tensor_scalar(mx[:, half(h)], proj[:, t, c0:c0 + 512], rs[:, t, h:h + 1], None, ALU.mult)
                ins.then_inc(mixed, 1)

            def stage_a(t):
                for h in range(2):
                    dve.wait_ge(hi_a, 2 * t + h + 1)
                    k = slice(4 * h, 4 * h + 4)
                    nc.vector.tensor_tensor(ml[t % 2][:, k, :], ta[h][:].rearrange("p (k c) -> p k c", k=4),
                                            mh[t % 2][:, k, :].bitcast(F32), ALU.subtract).then_inc(lo_a, 1)

            def stage_b(t):
                dve.wait_ge(x_in[t % 2], 16 * (t // 2 + 1))
                dve.wait_ge(multiplied, t + 1)
                if t >= 2:
                    dve.wait_ge(stored[t % 2], 32 * (t // 2))
                nc.vector.tensor_tensor(x1[:, t % 2, :], acc[:].rearrange("p h c -> p (h c)"), xt[:, t % 2, :], ALU.add).then_inc(x1_ok, 1)

            def stage_c(t):
                dve.wait_ge(sq_c, t + 1)
                nc.vector.tensor_scalar(ms2[:, t:t + 1], ss2[:, t:t + 1], 1.0 / D, EPS, ALU.mult, ALU.add).then_inc(ms_c, 1)
                dve.wait_ge(rs_c, t + 1)
                dve.wait_ge(x1_ok, t + 1)
                nc.vector.scalar_tensor_tensor(out=hn[:, t % 2, :], in0=x1[:, t % 2, :], scalar=rs2[:, t:t + 1], in1=g2[:],
                                               op0=ALU.mult, op1=ALU.mult).then_inc(hn_ok, 1)
                dve.wait_ge(logits, t + 1)
                nc.vector.tensor_reduce(nmax[:, t:t + 1], lg[:, 0:E], AX, ALU.max, negate=True).then_inc(maxed, 1)
                dve.wait_ge(exped, t + 1)
                nc.vector.reciprocal(rden[:, t:t + 1], den[:, t:t + 1]).then_inc(recip, 1)
                dve.wait_ge(recip, t + 1)
                nc.vector.tensor_scalar(aff[:], ex[:], rden[:, t:t + 1], None, ALU.mult).then_inc(aff_ok, 1)
                dve.wait_ge(aff_turned, t + 1)
                nc.vector.tensor_copy(affT[:, t * P:(t + 1) * P], at[0:E, 0:P]).then_inc(affT_ok, 1)

            for k in range(KD):
                dve.wait_ge(wo_hi, k + 1)
                nc.vector.scalar_tensor_tensor(out=wol[:, k, :], in0=wo32[:, k % 2, :], scalar=go[:, k:k + 1],
                                               in1=woh[:, k, :].bitcast(F32), op0=ALU.mult, op1=ALU.subtract).then_inc(wo_lo, 1)
                if k == 0:
                    normalise(0)
            for t in range(NT + 2):
                if t < NT:
                    stage_a(t)
                if t + 1 < NT:
                    normalise(t + 1)
                if 1 <= t <= NT:
                    stage_b(t - 1)
                if t >= 2:
                    stage_c(t - 2)
            dve.wait_ge(affT_ok, NT)

        @block.tensor
        def _(pe):
            pe.wait_ge(small_in, 64)

            def stage_a(t):
                pe.wait_ge(mixed, t + 1)
                for h in range(2):
                    if t:
                        pe.wait_ge(lo_a, 2 * t + h - 1)
                    for k in range(4):
                        c = (4 * h + k) * P
                        ins = nc.tensor.transpose(ta[h][:, k * P:(k + 1) * P], mx[:, c:c + P], ident[:])
                    ins.then_inc(turned_a, 1)

            def stage_b(t):
                pe.wait_ge(lo_a, 2 * t + 2)
                pe.wait_ge(wo_lo, KD)
                if t:
                    pe.wait_ge(x1_ok, t)
                for h in range(2):
                    for k in range(KD):
                        for m, (x, w) in enumerate(((mh, woh), (mh, wol), (ml, woh))):
                            ins = nc.tensor.matmul(acc[:, h, :], x[t % 2][:, k, :], w[:, k, half(h)],
                                                   start=(k == 0 and m == 0), stop=(k == KD - 1 and m == 2))
                ins.then_inc(multiplied, 1)

            def stage_c(t):
                pe.wait_ge(hn_ok, t + 1)
                for h in range(2):
                    if t:
                        pe.wait_ge(copied_c, 2 * t + h - 1)
                    for k in range(4):
                        c = (4 * h + k) * P
                        ins = nc.tensor.transpose(tc[h][:, k * P:(k + 1) * P], hn[:, t % 2, c:c + P], ident[:])
                    ins.then_inc(turned_c, 1)

            def route(t):
                pe.wait_ge(copied_c, 2 * t + 2)
                if t:
                    pe.wait_ge(exped, t)
                for k in range(KD):
                    ins = nc.tensor.matmul(lg[:, 0:E], hT[:, k, :], wr[:, k, :], start=(k == 0), stop=(k == KD - 1))
                ins.then_inc(logits, 1)
                pe.wait_ge(aff_ok, t + 1)
                if t:
                    pe.wait_ge(affT_ok, t)
                nc.tensor.transpose(at[0:E, 0:P], aff[:], ident[:]).then_inc(aff_turned, 1)

            for t in range(NT + 2):
                if t < NT:
                    stage_a(t)
                if 1 <= t <= NT:
                    stage_b(t - 1)
                if t >= 2:
                    stage_c(t - 2)
                    route(t - 2)


HF = FE // 2
HT = HF // P
NGU = 4 * (KD // 2)
NDN = FE // P // 2
NCH = NGU + NDN
CW = 2 * HF
DW = 2 * D
RING = 6
SPLIT = 3
NCOL = ((0, 512), (512, 512), (1024, 384))
BATCH = ((0, 4), (4, 4), (8, 3))


def experts(nc, d, keep):
    ident, affT = keep["ident"], keep["affT"]
    with ExitStack() as ctx:
        sb = lambda name, shape, dt=F32: ctx.enter_context(nc.sbuf_tensor(name, shape, dt))
        ps = lambda name, shape: ctx.enter_context(nc.psum_tensor(name, shape, F32))
        sem = lambda name: ctx.enter_context(nc.semaphore(name))
        vals, idxs, idxf = sb("e_vals", [E, CAP]), sb("e_idxs", [E, CAP], U32), sb("e_idxf", [E, CAP])
        gates, idxT = sb("e_gates", [P, E]), sb("e_idxT", [P, E], U32)
        idx = [sb(f"e_idx{b}", [P, 1], U32) for b in range(2)]
        xg = sb("e_xg", [P, D])
        xh, xl = sb("e_xh", [P, KD, P], F32R), sb("e_xl", [P, KD, P], F32R)
        raw = [sb(f"e_raw{s}", [P, CW]) for s in range(RING)]
        wh = [sb(f"e_wh{b}", [P, CW], F32R) for b in range(SPLIT)]
        wl = [sb(f"e_wl{b}", [P, CW], F32R) for b in range(SPLIT)]
        gate = sb("e_gate", [P, HF])
        hid = sb("e_hid", [P, HF])
        hh, hl = sb("e_hh", [P, 2 * HT, P], F32R), sb("e_hl", [P, 2 * HT, P], F32R)
        y = sb("e_y", [P, 2, D])
        acc = [ps(f"e_acc{b}", [P, 3, 512]) for b in range(2)]
        turn = [ps(f"e_turn{b}", [P, 512]) for b in range(2)]
        top, top_turned, top_ok = sem("e_top"), sem("e_top_turned"), sem("e_top_ok")
        raw_in = [sem(f"e_raw_in{s}") for s in range(RING)]
        hi_ok, lo_ok, used = sem("e_hi_ok"), sem("e_lo_ok"), sem("e_used")
        idx_ok, gathered, added = sem("e_idx_ok"), sem("e_gathered"), sem("e_added")
        x_turned = sem("e_x_turned")
        full, hi_t, lo_t = sem("e_full"), sem("e_hi_t"), sem("e_lo_t")
        y_free = sem("e_y_free")
        passed, sp_passed = sem("e_passed"), sem("e_sp_passed")
        silu_ok, hid_ok, y_ok = sem("e_silu_ok"), sem("e_hid_ok"), sem("e_y_ok")
        block = ctx.enter_context(nc.Block())

        views = {n: d[n][0].rearrange("e (c k p) f -> e c p k f", k=2, p=P) for n in ("w_gate", "w_up", "w_down")}

        def source(e, n):
            if n >= NGU:
                return views["w_down"][e, n - NGU]
            h, which, c = n // 8, n // 4 % 2, n % 4
            return views["w_up" if which else "w_gate"][e, c][:, :, h * HF:(h + 1) * HF]

        def slot(buf, n):
            w = DW if n >= NGU else CW
            return buf[:, 0:w]

        def pairs(eng, body):
            body(0, True, False)
            with eng.Fori(1, E // 2 - 1) as i:
                body(i, False, False)
            body(E // 2 - 1, False, True)

        def at_chunk(i, m, back=0):
            v = 2 * NCH * i + m + 1 - back
            return None if isinstance(i, int) and v < 1 else v

        def wait(eng, s, v):
            if v is not None:
                eng.wait_ge(s, v)

        TURNS = [(10, 0, b) for b in range(3)] + [(18, 1, b) for b in range(3)] + [(22, 2, b) for b in range(2)]
        BATCHES = {at + b: (n, half, b) for n, (at, half, b) in enumerate(TURNS)}

        def turned_to(half, b):
            if half == 2:
                return xh[:, 4 * b:4 * b + 4, :], xl[:, 4 * b:4 * b + 4, :], 4
            first, n = BATCH[b]
            t = slice(half * HT + first, half * HT + first + n)
            return hh[:, t, :], hl[:, t, :], n

        def nth_turn(i, par, n):
            return 2 + (2 * i + par) * len(TURNS) + n

        def n_of(m):
            return m % NCH

        def later(i, m, take_turn, silu=None, hidden=None, result=None):
            if m < 2:
                return later_of(i, 1, m + NCH - 2, take_turn, silu, hidden, result, back=True)
            par, n = divmod(m - 2, NCH)
            return later_of(i, par, n, take_turn, silu, hidden, result, back=False)

        def later_of(i, par, n, take_turn, silu, hidden, result, back):
            if back:
                if isinstance(i, int) and i == 0:
                    return
                i = i - 1
            if n in (3, 11) and silu:
                silu(i, par, n // 8)
            if n in (7, 15) and hidden:
                hidden(i, par, n // 8)
            if n == NCH - 1 and result:
                result(i, par)
            if n in BATCHES:
                turn_no, half, b = BATCHES[n]
                if not (half == 2 and par == 1 and isinstance(i, int) and i == E // 2 - 1):
                    take_turn(i, par, turn_no, half, b)

        @block.sync
        def _(sp):
            for m in range(RING):
                sp.dma_start(slot(raw[m], m).rearrange("p (k f) -> p k f", k=2), source(0, m)).then_inc(raw_in[m], 16)

            def body(i, first, last):
                for m in range(2 * NCH - (RING if last else 0)):
                    sp.wait_ge(lo_ok, at_chunk(i, m))
                    sp.sem_inc(sp_passed, 1)
                    par, n = divmod(m + RING, NCH)
                    sp.dma_start(slot(raw[m % RING], n).rearrange("p (k f) -> p k f", k=2),
                                 source(2 * i + par, n)).then_inc(raw_in[m % RING], 16)

            with sp.Fori(0, E // 2 - 1) as i:
                body(i, False, False)
            body(E // 2 - 1, False, True)

        @block.gpsimd
        def _(pool):
            def gather(e, b, n):
                nc.gpsimd.tensor_copy(idx[b][:], idxT[:, bass.ds(e, 1)]).then_inc(idx_ok, 1)
                pool.wait_ge(idx_ok, n + 1)
                pool.sem_inc(passed, 1)
                nc.gpsimd.indirect_dma_start(out=xg[:], out_offset=None, in_=d["hn"],
                                             in_offset=bass.IndirectOffsetOnAxis(ap=idx[b][:], axis=0)).then_inc(gathered, 16)

            def body(i, first, last):
                for par in range(2):
                    e = 2 * i + par
                    if not (first and par == 0):
                        pool.wait_ge(added, 16 * e)
                        pool.sem_inc(y_free, 1)
                    if not (last and par):
                        pool.wait_ge(x_turned, e + 1)
                        gather(e + 1, 1 - par, e + 1)
                    pool.wait_ge(y_ok, e + 1)
                    pool.sem_inc(passed, 1)
                    nc.gpsimd.indirect_dma_start(out=d["out"], out_offset=bass.IndirectOffsetOnAxis(ap=idx[par][:], axis=0),
                                                 in_=y[:, par, :], in_offset=None, compute_op=ALU.add).then_inc(added, 16)

            pool.sem_inc(y_free, 2)
            pool.wait_ge(top_ok, 2)
            gather(0, 0, 0)
            pairs(pool, body)
            pool.wait_ge(added, 16 * E)

        @block.scalar
        def _(act):
            def take_turn(i, par, n, half, b):
                hi, lo, w = turned_to(half, b)
                u = nth_turn(i, par, n)
                act.wait_ge(full, u + 1)
                nc.scalar.copy(hi, turn[n % 2][:, 0:w * P].rearrange("p (k c) -> p k c", k=w)).then_inc(hi_t, 1)

            def silu(i, par, half):
                e = 2 * i + par
                act.wait_ge(used, at_chunk(i, par * NCH + 8 * half + 3))
                if not (half == 0 and isinstance(i, int) and i == 0 and par == 0):
                    act.wait_ge(hid_ok, 2 * e + half)
                nc.scalar.activation(gate[:, 0:1024], acc[par][:, 0:2, :].rearrange("p a c -> p (a c)"), ACT.Silu)
                nc.scalar.activation(gate[:, 1024:HF], acc[par][:, 2, 0:HF - 1024], ACT.Silu).then_inc(silu_ok, 1)

            def body(i, first, last):
                for m in range(2 * NCH):
                    act.wait_ge(raw_in[m % RING], 16 * (2 * NCH // RING * i + m // RING + 1))
                    wait(act, used, at_chunk(i, m, SPLIT))
                    nc.scalar.copy(slot(wh[m % SPLIT], n_of(m)), slot(raw[m % RING], n_of(m))).then_inc(hi_ok, 1)
                    later(i, m, take_turn, silu)

            for b in range(2):
                act.wait_ge(full, b + 1)
                hi, lo, w = turned_to(2, b)
                nc.scalar.copy(hi, turn[b][:].rearrange("p (k c) -> p k c", k=w)).then_inc(hi_t, 1)
            pairs(act, body)

        @block.vector
        def _(dve):
            own = Chain(dve, top)
            for r in range(CAP // 8):
                v = vals[:, 8 * r:8 * r + 8]
                own.link(nc.vector.max(v, affT[:]))
                own.link(nc.vector.max_index(idxs[:, 8 * r:8 * r + 8], v, affT[:]))
                own.link(nc.vector.match_replace(affT[:], v, affT[:], -1.0))
            own.link(nc.vector.tensor_copy(idxf[:], idxs[:]))
            dve.wait_ge(top_turned, 1)
            nc.vector.tensor_copy(gates[:], turn[0][:, 0:E]).then_inc(top_ok, 1)
            nc.vector.tensor_copy(idxT[:], turn[0][:, E:2 * E]).then_inc(top_ok, 1)
            for b in range(2):
                dve.wait_ge(hi_t, b + 1)
                hi, lo, w = turned_to(2, b)
                nc.vector.tensor_tensor(lo, turn[b][:].rearrange("p (k c) -> p k c", k=w), hi.bitcast(F32), ALU.subtract).then_inc(lo_t, 1)

            def take_turn(i, par, n, half, b):
                hi, lo, w = turned_to(half, b)
                dve.wait_ge(hi_t, nth_turn(i, par, n) + 1)
                nc.vector.tensor_tensor(lo, turn[n % 2][:, 0:w * P].rearrange("p (k c) -> p k c", k=w), hi.bitcast(F32),
                                        ALU.subtract).then_inc(lo_t, 1)

            def hidden(i, par, half):
                e = 2 * i + par
                dve.wait_ge(used, at_chunk(i, par * NCH + 8 * half + 7))
                dve.wait_ge(silu_ok, 2 * e + half + 1)
                a = acc[1 - par]
                nc.vector.tensor_tensor(hid[:, 0:1024], gate[:, 0:1024], a[:, 0:2, :].rearrange("p a c -> p (a c)"), ALU.mult)
                nc.vector.tensor_tensor(hid[:, 1024:HF], gate[:, 1024:HF], a[:, 2, 0:HF - 1024], ALU.mult).then_inc(hid_ok, 1)

            def result(i, par):
                e = 2 * i + par
                dve.wait_ge(used, at_chunk(i, par * NCH + NCH - 1))
                dve.wait_ge(y_free, e + 1)
                nc.vector.tensor_scalar(y[:, par, :], acc[par][:, 0:2, :].rearrange("p a c -> p (a c)"),
                                        gates[:, bass.ds(e, 1)], None, ALU.mult).then_inc(y_ok, 1)

            def body(i, first, last):
                for m in range(2 * NCH + 2):
                    if m < 2 * NCH:
                        dve.wait_ge(hi_ok, at_chunk(i, m))
                        nc.vector.tensor_tensor(slot(wl[m % SPLIT], n_of(m)), slot(raw[m % RING], n_of(m)),
                                                slot(wh[m % SPLIT], n_of(m)).bitcast(F32), ALU.subtract).then_inc(lo_ok, 1)
                    elif not last:
                        continue
                    else:
                        wait(dve, used, at_chunk(i, m, 2))
                    later(i, m, take_turn, None, hidden, result)

            pairs(dve, body)

        @block.tensor
        def _(pe):
            pe.wait_ge(top, 3 * CAP // 8 + 1)
            nc.tensor.transpose(turn[0][:, 0:E], vals[:], ident[0:E, 0:E])
            nc.tensor.transpose(turn[0][:, E:2 * E], idxf[:], ident[0:E, 0:E]).then_inc(top_turned, 1)
            pe.wait_ge(gathered, 16)
            pe.wait_ge(top_ok, 2)
            for b in range(2):
                for k in range(4):
                    c = (4 * b + k) * P
                    ins = nc.tensor.transpose(turn[b][:, k * P:(k + 1) * P], xg[:, c:c + P], ident[:])
                ins.then_inc(full, 1)
            pe.wait_ge(full, 2)
            pe.sem_inc(x_turned, 1)

            def turn_batch(i, par, no, half, b):
                e = 2 * i + par
                u = nth_turn(i, par, no)
                if half == 2:
                    if b == 0:
                        pe.wait_ge(gathered, 16 * (e + 2))
                    for k in range(4):
                        c = (4 * b + k) * P
                        ins = nc.tensor.transpose(turn[no % 2][:, k * P:(k + 1) * P], xg[:, c:c + P], ident[:])
                else:
                    if b == 0:
                        pe.wait_ge(hid_ok, 2 * e + half + 1)
                    first, w = BATCH[b]
                    for k in range(w):
                        c = (first + k) * P
                        ins = nc.tensor.transpose(turn[no % 2][:, k * P:(k + 1) * P], hid[:, c:c + P], ident[:])
                ins.then_inc(full, 1)
                if half == 2 and b == 1:
                    pe.wait_ge(full, u + 1)
                    pe.sem_inc(x_turned, 1)

            def before_chunk(i, par, n):
                e = 2 * i + par
                if n == 0:
                    pe.wait_ge(lo_t, nth_turn(i, par, 0))
                if n == 4 and not (isinstance(i, int) and i == 0 and par == 0):
                    pe.wait_ge(y_ok, e)
                if n == 8:
                    pe.wait_ge(silu_ok, 2 * e + 1)
                if n == 12:
                    pe.wait_ge(hid_ok, 2 * e + 1)
                if n == NGU:
                    pe.wait_ge(silu_ok, 2 * e + 2)
                    pe.wait_ge(lo_t, nth_turn(i, par, 2) + 1)
                for b in range(3):
                    if n == NGU + (HT + BATCH[b][0]) // 2:
                        pe.wait_ge(lo_t, nth_turn(i, par, 3 + b) + 1)

            def body(i, first, last):
                for m in range(2 * NCH):
                    par, n = divmod(m, NCH)
                    before_chunk(i, par, n)
                    pe.wait_ge(lo_ok, at_chunk(i, m))
                    a = acc[(5 * par + (n // 4 if n < NGU else 4)) % 2]
                    for k in range(2):
                        if n < NGU:
                            kt, base, cols, ops = 2 * (n % 4) + k, k * HF, NCOL, (xh, xl)
                            start, stop = kt == 0, kt == KD - 1
                        else:
                            kt, base, cols, ops = 2 * (n - NGU) + k, k * D, ((0, 512), (512, 512)), (hh, hl)
                            start, stop = kt == 0, kt == 2 * HT - 1
                        for s, (x, w) in enumerate(((ops[0], wh), (ops[0], wl), (ops[1], wh))):
                            for c, (c0, cw) in enumerate(cols):
                                ins = nc.tensor.matmul(a[:, c, 0:cw], x[:, kt, :], w[m % SPLIT][:, base + c0:base + c0 + cw],
                                                       start=(start and s == 0), stop=(stop and s == 2))
                    ins.then_inc(used, 1)
                    if n in BATCHES:
                        turn_no, half, b = BATCHES[n]
                        if not (half == 2 and par == 1 and last):
                            if turn_no >= 0:
                                pe.wait_ge(lo_t, nth_turn(i, par, turn_no) - 1)
                            turn_batch(i, par, turn_no, half, b)

            pairs(pe, body)


def build(nc, d):
    with ExitStack() as ctx:
        keep = {
            "ident": ctx.enter_context(nc.sbuf_tensor("ident_sb", [P, P], F32)),
            "affT": ctx.enter_context(nc.sbuf_tensor("affT", [E, S], F32)),
        }
        with ExitStack() as front:
            keep["proj"] = front.enter_context(nc.sbuf_tensor("proj", [P, NT, INW], F32))
            project(nc, d, keep)
            attend(nc, d, keep)
            mix(nc, d, keep)
        experts(nc, d, keep)


NAMES = ["x", "norm1_g", "w_in", "na_q_norm_g", "na_k_norm_g", "gqa_q_norm_g", "gqa_k_norm_g",
         "na_out_g", "gqa_out_g", "w_out", "norm2_g", "w_router", "w_gate", "w_up", "w_down"]


def kernel(**inputs):
    import concourse.bacc as bacc
    from concourse.bass_utils import run_bass_kernel_spmd

    arrays = {n: np.ascontiguousarray(inputs[n]) for n in NAMES}
    rpb = np.asarray(inputs["na_rpb"])[0]
    side = (PAD_W - rpb.shape[-1]) // 2
    arrays["rpb"] = np.ascontiguousarray(np.pad(rpb, ((0, 0), (0, 0), (side, side))))
    arrays.update(constants())
    nc = bacc.Bacc("TRN2", target_bir_lowering=False, num_devices=1)
    d = {n: nc.dram_tensor(f"in_{n}", a.shape, mybir.dt.from_np(a.dtype), kind="ExternalInput").ap() for n, a in arrays.items()}
    d["out"] = nc.dram_tensor("out_0", (S, D), F32, kind="ExternalOutput").ap()
    d["hn"] = nc.dram_tensor("hn", (S, D), F32, kind="Internal").ap()
    d["rows"] = nc.dram_tensor("rows", (NH, 15, GRID_W, PAD_W), F32, kind="Internal").ap()
    build(nc, d)
    got = run_bass_kernel_spmd(nc, [{f"in_{n}": a for n, a in arrays.items()}], core_ids=[0])
    return got.results[0]["out_0"].reshape(1, S, D)
```

```python
from contextlib import ExitStack

import concourse.bass as bass
import numpy as np
from concourse import mybir
from concourse.alu_op_type import AluOpType as ALU

ACT = mybir.ActivationFunctionType
AX = mybir.AxisListType.X
F32, F32R, U32 = mybir.dt.float32, mybir.dt.float32r, mybir.dt.uint32

P = 128
S = D = 1024
NT = S // P
KD = D // P
HD = 64
GRID_W = 64
NH = 8
KVH = 2
NQ0, NK0, NV0 = 0, 512, 1024
GQ0, GK0, GV0 = 1536, 2048, 2176
INW = 2304
GW = 256
NG = INW // GW
E, CAP, FE = 16, 128, 2816
EPS = 1e-6
NEG = -1e30
PAD_W = 2 * GRID_W - 1
BW = 7 * P
B0 = 32
WO_RING = 6
IW = 5 * P


def key_tiles(t):
    if t < 2:
        return 0, 4
    if t > 5:
        return 4, 4
    return t - 2, 5


def constants():
    tok = np.arange(S)
    inv = (1.0 / (10000.0 ** (np.arange(0, 32, 2, dtype=np.float32) / np.float32(32)))).astype(np.float32)
    row, col = (tok // GRID_W).astype(np.float32), (tok % GRID_W).astype(np.float32)
    ang = np.concatenate([row[:, None] * inv[None], col[:, None] * inv[None]], -1)
    cos, sin = np.cos(ang), np.sin(ang)
    cc = np.repeat(cos, 2, -1)
    ss = np.stack([-sin, sin], -1).reshape(S, HD)
    rope = np.stack([cc, ss]).astype(np.float32)
    c = np.arange(GRID_W)
    start = np.clip(c - 8, 0, GRID_W - 16)
    ok = (c[None, :] >= start[:, None]) & (c[None, :] < start[:, None] + 16)
    qr = np.arange(2)
    rr = np.arange(-6, 8)
    wide = np.broadcast_to(ok[None, :, None, :], (2, 64, 14, 64))
    dr = rr[None, :] - qr[:, None]
    rows_ok = ((dr >= -4) & (dr <= 3))[:, None, :, None]
    inner = (wide & rows_ok)[:, :, 2:12]
    mask = np.concatenate([wide.reshape(P, BW), inner.reshape(P, IW)], -1)
    return {
        "ident": np.eye(P, dtype=np.float32),
        "rope": rope,
        "mask": np.where(mask, 0.0, NEG).astype(np.float32),
    }


class Chain:

    def __init__(self, eng, sem, base=0):
        self.eng, self.sem, self.base, self.n = eng, sem, base, 0

    def link(self, ins):
        self.n += 1
        ins.then_inc(self.sem, 1)
        self.eng.wait_ge(self.sem, self.base + self.n)


class Prep:

    def __init__(self, nc, ctx):
        sb = lambda name, shape: ctx.enter_context(nc.sbuf_tensor(name, shape, F32))
        sem = lambda name: ctx.enter_context(nc.semaphore(name))
        self.gains = sb("a_gains", [P, 4, HD])
        self.ssq = sb("a_ssq", [P, 2, NT, 2])
        self.rs = sb("a_rs", [P, 2, NT, 2])
        self.pw = sb("a_pow", [P, 2 * NT])
        self.qk = sb("a_qk", [P, 2, NT, P])
        self.gain_in, self.setup = sem("a_gain_in"), sem("a_setup")
        self.pool_own, self.dve_own = sem("a_pool_own"), sem("a_dve_own")
        self.squared, self.reduced, self.ready = sem("a_squared"), sem("a_reduced"), sem("a_ready")
        self.qk_turned, self.passed = sem("a_qk_turned"), sem("a_passed")


def set_up(nc, pool, a):
    nc.gpsimd.memset(a.pw[:], -0.5).then_inc(a.setup, 1)
    pool.wait_ge(a.gain_in, 64)
    for n in (0, 2):
        ins = nc.gpsimd.tensor_scalar(a.gains[:, n, :], a.gains[:, n, :], HD ** -0.5, None, ALU.mult)
    ins.then_inc(a.setup, 1)
    pool.wait_ge(a.setup, 2)


def square_head(nc, pool, a, squares, qc, kc):
    sq = squares[:].rearrange("p (t c) -> p t c", t=NT)
    pool.sem_inc(a.passed, 1)
    nc.gpsimd.tensor_tensor(sq[:, :, 0:HD], qc, qc, ALU.mult)
    nc.gpsimd.tensor_tensor(sq[:, :, HD:P], kc, kc, ALU.mult).then_inc(a.squared, 1)


def normalise_head(nc, pool, a, own, qc, kc, kind, j, b, first):
    dst = a.qk[:, b]
    pool.wait_ge(a.reduced, j + 1)
    own.link(nc.gpsimd.tensor_tensor(a.rs[:, b].rearrange("p t w -> p (t w)"),
                                     a.ssq[:, b].rearrange("p t w -> p (t w)"), a.pw[:], ALU.pow))
    if not first:
        pool.wait_ge(a.qk_turned, 2 * j - 2)
        pool.sem_inc(a.passed, 1)
    for w, c in enumerate((qc, kc)):
        ins = nc.gpsimd.tensor_tensor(dst[:, :, w * HD:(w + 1) * HD], c,
                                      a.rs[:, b, :, w:w + 1].to_broadcast([P, NT, HD]), ALU.mult)
    own.link(ins)
    for w in range(2):
        part = dst[:, :, w * HD:(w + 1) * HD]
        ins = nc.gpsimd.tensor_tensor(part, part, a.gains[:, 2 * kind + w, :].unsqueeze(1).to_broadcast([P, NT, HD]), ALU.mult)
    return ins


def sum_squares(nc, dve, a, squares, own, j, b):
    dve.wait_ge(a.squared, j + 1)
    flat = a.ssq[:, b].rearrange("p t w -> p (t w)")
    own.link(nc.vector.tensor_reduce(flat, squares[:].rearrange("p (n c) -> p n c", c=HD), AX, ALU.add))
    nc.vector.tensor_scalar(flat, flat, 1.0 / HD, EPS, ALU.mult, ALU.add).then_inc(a.reduced, 1)


def project(nc, d, keep):
    proj, ident, sq, prep = keep["proj"], keep["ident"], keep["squares"], keep["prep"]
    with ExitStack() as ctx:
        sb = lambda name, shape, dt=F32: ctx.enter_context(nc.sbuf_tensor(name, shape, dt))
        ps = lambda name, shape: ctx.enter_context(nc.psum_tensor(name, shape, F32))
        sem = lambda name: ctx.enter_context(nc.semaphore(name))
        xt = sb("p_x", [P, 2, D])
        ss = sb("p_ss", [P, NT])
        ms = sb("p_ms", [P, NT])
        rstd = sb("p_rstd", [P, NT])
        pw = sb("p_pow", [P, NT])
        g1 = sb("p_g1", [P, KD])
        xh = sb("p_xh", [P, KD, S], F32R)
        xl = sb("p_xl", [P, KD, S], F32R)
        w32 = sb("p_w32", [P, 2, KD, GW])
        wh = sb("p_wh", [P, 2, KD, GW], F32R)
        wl = sb("p_wl", [P, 2, KD, GW], F32R)
        tp = [ps(f"p_tp{b}", [P, 512]) for b in range(4)]
        acc = [ps(f"p_acc{b}", [P, 512]) for b in range(4)]
        x_in = [sem(f"p_x_in{b}") for b in range(2)]
        ident_in, gain_in = sem("p_ident_in"), sem("p_gain_in")
        w_in = [sem(f"p_w_in{b}") for b in range(2)]
        squared, rows_out = sem("p_squared"), sem("p_rows_out")
        means = sem("p_means")
        powc = sem("p_powc")
        rstd_ok = sem("p_rstd_ok")
        turned = sem("p_turned")
        x_hi, x_lo = sem("p_x_hi"), sem("p_x_lo")
        w_hi, w_lo = sem("p_w_hi"), sem("p_w_lo")
        acc_full = sem("p_acc_full")
        acc_act, acc_dve = sem("p_acc_act"), sem("p_acc_dve")
        block = ctx.enter_context(nc.Block())

        w_src = d["w_in"][0].rearrange("(k p) n -> p k n", p=P)

        @block.sync
        def _(sp):
            def load_group(n):
                if n >= 2:
                    sp.wait_ge(w_lo, 2 * (n - 1))
                sp.dma_start(w32[:, n % 2], w_src[:, :, n * GW:(n + 1) * GW]).then_inc(w_in[n % 2], 16)

            sp.dma_start(ident[:], d["ident"]).then_inc(ident_in, 16)
            for t in range(NT):
                if t >= 2:
                    sp.wait_ge(squared, t - 1)
                    sp.wait_ge(turned, 2 * (t - 1))
                sp.dma_start(xt[:, t % 2, :], d["x"][0, t * P:(t + 1) * P, :]).then_inc(x_in[t % 2], 16)
                if t == 0:
                    with nc.allow_non_contiguous_dma(reason="a gain vector by partition, once"):
                        sp.dma_start(g1[:], d["norm1_g"][0].rearrange("(k p) -> p k", p=P)).then_inc(gain_in, 16)
                    load_group(0)
                if t == 3:
                    load_group(1)
            for n, name in enumerate(("na_q_norm_g", "na_k_norm_g", "gqa_q_norm_g", "gqa_k_norm_g")):
                sp.dma_start(prep.gains[:, n, :], d[name].to_broadcast([P, HD])).then_inc(prep.gain_in, 16)
            for n in range(2, NG):
                load_group(n)
                for h in ((n - 2,) if n < NG - 1 else (n - 2, n - 1)):
                    sp.dma_start(d["rows"][h], d["rpb"][h].unsqueeze(1).to_broadcast([15, GRID_W, PAD_W])).then_inc(rows_out, 16)
            sp.wait_ge(rows_out, 16 * NH)

        @block.gpsimd
        def _(pool):
            nc.gpsimd.memset(pw[:], -0.5).then_inc(powc, 1)
            pool.wait_ge(powc, 1)
            for t in range(NT):
                pool.wait_ge(means, t + 1)
                nc.gpsimd.tensor_tensor(rstd[:, t:t + 1], ms[:, t:t + 1], pw[:, 0:1], ALU.pow).then_inc(rstd_ok, 1)
            set_up(nc, pool, prep)
            pool.wait_ge(acc_act, 3 * NT // 2)
            pool.wait_ge(acc_dve, 3 * NT // 2)
            for h in range(2):
                own = Chain(pool, prep.pool_own, 3 * h)
                qc, kc = (proj[:, :, c + h * HD:c + (h + 1) * HD] for c in (NQ0, NK0))
                square_head(nc, pool, prep, keep["squares"], qc, kc)
                own.link(normalise_head(nc, pool, prep, own, qc, kc, 0, h, h, True))
                pool.sem_inc(prep.ready, 1)

        @block.scalar
        def _(act):
            def split_hi(n):
                act.wait_ge(w_in[n % 2], 16 * (n // 2 + 1))
                if n >= 2:
                    act.wait_ge(acc_full, (n - 1) * NT)
                for k in range(KD):
                    ins = nc.scalar.activation(wh[:, n % 2, k, :], w32[:, n % 2, k, :], ACT.Copy, scale=g1[:, k:k + 1])
                    if k % (KD // 2) == KD // 2 - 1:
                        ins.then_inc(w_hi, 1)

            def read_out(n, t):
                act.wait_ge(acc_full, n * NT + t + 1)
                nc.scalar.activation(proj[:, t, n * GW:(n + 1) * GW], acc[t % 4][:, 0:GW], ACT.Copy,
                                     scale=rstd[:, t:t + 1]).then_inc(acc_act, 1)

            for t in range(NT):
                act.wait_ge(x_in[t % 2], 16 * (t // 2 + 1))
                if t:
                    act.wait_ge(squared, t)
                nc.scalar.activation(sq[:], xt[:, t % 2, :], ACT.Square, accum_out=ss[:, t:t + 1]).then_inc(squared, 1)
                for h in range(2):
                    act.wait_ge(turned, 2 * t + h + 1)
                    nc.scalar.copy(xh[:, 4 * h:4 * h + 4, t * P:(t + 1) * P],
                                   tp[(2 * t + h) % 4][:].rearrange("p (k c) -> p k c", k=4)).then_inc(x_hi, 1)
                if t == 0:
                    act.wait_ge(gain_in, 16)
                    split_hi(0)
                if t == 5:
                    split_hi(1)
                if t >= 2 and t % 2 == 0:
                    act.wait_ge(rstd_ok, t - 1)
                    read_out(0, t - 2)
            act.wait_ge(rstd_ok, NT)
            for n in range(NG):
                for t in range(0 if n else NT - 2, NT, 2):
                    read_out(n, t)
                if n + 2 < NG:
                    split_hi(n + 2)
            act.wait_ge(acc_act, NG * NT // 2)

        @block.vector
        def _(dve):
            def split_lo(n):
                for k in range(KD):
                    if k % (KD // 2) == 0:
                        dve.wait_ge(w_hi, 2 * n + 1 + k // (KD // 2))
                    ins = nc.vector.scalar_tensor_tensor(out=wl[:, n % 2, k, :], in0=w32[:, n % 2, k, :], scalar=g1[:, k:k + 1],
                                                         in1=wh[:, n % 2, k, :].bitcast(F32), op0=ALU.mult, op1=ALU.subtract)
                    if k % (KD // 2) == KD // 2 - 1:
                        ins.then_inc(w_lo, 1)

            def read_out(n, t):
                dve.wait_ge(acc_full, n * NT + t + 1)
                nc.vector.tensor_scalar(proj[:, t, n * GW:(n + 1) * GW], acc[t % 4][:, 0:GW], rstd[:, t:t + 1],
                                        None, ALU.mult).then_inc(acc_dve, 1)

            for t in range(NT):
                for h in range(2):
                    dve.wait_ge(x_hi, 2 * t + h + 1)
                    cols = (slice(None), slice(4 * h, 4 * h + 4), slice(t * P, (t + 1) * P))
                    nc.vector.tensor_tensor(xl[cols], tp[(2 * t + h) % 4][:].rearrange("p (k c) -> p k c", k=4),
                                            xh[cols].bitcast(F32), ALU.subtract).then_inc(x_lo, 1)
                dve.wait_ge(squared, t + 1)
                nc.vector.tensor_scalar(ms[:, t:t + 1], ss[:, t:t + 1], 1.0 / D, EPS, ALU.mult, ALU.add).then_inc(means, 1)
                if t == 0:
                    dve.wait_ge(gain_in, 16)
                    split_lo(0)
                if t == 5:
                    split_lo(1)
                if t >= 3 and t % 2:
                    dve.wait_ge(rstd_ok, t - 1)
                    read_out(0, t - 2)
            dve.wait_ge(rstd_ok, NT)
            for n in range(NG):
                for t in range(1 if n else NT - 1, NT, 2):
                    read_out(n, t)
                if n + 2 < NG:
                    split_lo(n + 2)
                if n in (3, 4):
                    h = n - 3
                    sum_squares(nc, dve, prep, keep["squares"], Chain(dve, prep.dve_own, h), h, h)
            dve.wait_ge(acc_dve, NG * NT // 2)

        @block.tensor
        def _(pe):
            def product(t, b, first=False):
                cols = slice(t * P, (t + 1) * P)
                for k in range(KD):
                    if first and k % (KD // 2) == 0:
                        pe.wait_ge(w_lo, 1 + k // (KD // 2))
                    for m, (x, w) in enumerate(((xh, wh), (xh, wl), (xl, wh))):
                        ins = nc.tensor.matmul(acc[t % 4][:, 0:GW], x[:, k, cols], w[:, b, k, :],
                                               start=(k == 0 and m == 0), stop=(k == KD - 1 and m == 2))
                ins.then_inc(acc_full, 1)

            def group(n, b):
                pe.wait_ge(w_lo, 2 * n + 2)
                for t in range(NT):
                    pe.wait_ge(acc_dve if t % 2 else acc_act, 4 * n + t // 2 - 1)
                    product(t, b)

            for t in range(NT + 1):
                if t < NT:
                    if t == 0:
                        pe.wait_ge(ident_in, 16)
                    pe.wait_ge(x_in[t % 2], 16 * (t // 2 + 1))
                    for h in range(2):
                        if 2 * t + h >= 4:
                            pe.wait_ge(x_lo, 2 * t + h - 3)
                        for k in range(4):
                            ins = nc.tensor.transpose(tp[(2 * t + h) % 4][:, k * P:(k + 1) * P],
                                                      xt[:, t % 2, (4 * h + k) * P:(4 * h + k + 1) * P], ident[:])
                        ins.then_inc(turned, 1)
                if t:
                    u = t - 1
                    pe.wait_ge(x_lo, 2 * t)
                    if u >= 4:
                        pe.wait_ge(acc_dve if u % 2 else acc_act, u // 2 - 1)
                    product(u, 0, u == 0)
            with pe.Fori(0, (NG - 1) // 2) as i:
                group(2 * i + 1, 1)
                group(2 * i + 2, 0)


def attend(nc, d, keep):
    proj, ident, squares, prep = keep["proj"], keep["ident"], keep["squares"], keep["prep"]
    qk, qk_turned, passed, ready, pool_own, dve_own = (
        prep.qk, prep.qk_turned, prep.passed, prep.ready, prep.pool_own, prep.dve_own)
    with ExitStack() as ctx:
        sb = lambda name, shape, dt=F32: ctx.enter_context(nc.sbuf_tensor(name, shape, dt))
        ps = lambda name, shape: ctx.enter_context(nc.psum_tensor(name, shape, F32))
        sem = lambda name: ctx.enter_context(nc.semaphore(name))
        rope = sb("a_rope", [P, 2, NT, HD])
        mask = sb("a_mask", [P, BW + IW])
        raw = sb("a_raw", [P, 2, 14, GRID_W])
        bias = sb("a_bias", [P, 2, BW + IW])
        swp = sb("a_swp", [P, NT, P])
        q1 = [sb(f"a_q1{b}", [P, S], F32R) for b in range(2)]
        k1 = [sb(f"a_k1{b}", [P, S], F32R) for b in range(2)]
        k2 = [sb(f"a_k2{b}", [HD, S], F32R) for b in range(2)]
        negs = sb("a_negs", [P, 2, IW])
        negm = sb("a_negm", [P, 2, NT])
        rsum = sb("a_rsum", [P, 2, NT])
        rinv = sb("a_rinv", [P, NT])
        prob = sb("a_prob", [P, 2, S])
        probT = [sb(f"a_probT{b}", [P, S]) for b in range(2)]
        spsum = [ps(f"a_s{b}", [P, 2, 512]) for b in range(2)]
        turn = [ps(f"a_turn{b}", [P, 512]) for b in range(2)]
        opsum = [ps(f"a_o{b}", [P, NT, HD]) for b in range(2)]
        mask_in, rope_in = sem("a_mask_in"), sem("a_rope_in")
        raw_in = [sem(f"a_raw_in{b}") for b in range(2)]
        bias_ok = sem("a_bias_ok")
        hi_ok, qk_split = sem("a_hi_ok"), sem("a_qk_split")
        full = [sem(f"a_full{b}") for b in range(2)]
        free = [sem(f"a_free{b}") for b in range(2)]
        scored, maxed, exped, summed, o_free = sem("a_scored"), sem("a_maxed"), sem("a_exped"), sem("a_summed"), sem("a_o_free")
        block = ctx.enter_context(nc.Block())
        NA, GQ = 0, 1
        TURN_AT = {1: 0, 3: 1}
        SUMS_AT = {NA: 1, GQ: 2}

        def tiles(kind, t):
            return (0, NT) if kind == GQ else key_tiles(t)

        def wide(kind, upto=NT):
            return sum(tiles(kind, s)[1] > 4 for s in range(upto))

        def before(kind, h, b):
            if b == 0:
                return NT * (h + NH * kind)
            return wide(NA) * h if kind == NA else wide(NA) * NH + wide(GQ) * h

        def use(kind, h, b, t):
            return before(kind, h, b) + (t + 1 if b == 0 else wide(kind, t + 1))

        def ahead(kind, h, b, t, nxt):
            if t < NT:
                return kind, h, b, t
            return None if nxt is None else (nxt, 0 if nxt != kind else h + 1, 1 - b, t - NT)

        def heads(eng, body):
            for kind in (NA, GQ):
                with eng.Fori(0, NH // 2 - 1) as i:
                    for b in range(2):
                        body(kind, 2 * i + b, b, kind)
                body(kind, NH - 2, 0, kind)
                body(kind, NH - 1, 1, GQ if kind == NA else None)

        def step_of(kind, h, t):
            return (h + NH * kind) * NT + t

        @block.sync
        def _(sp):
            sp.dma_start(mask[:], d["mask"]).then_inc(mask_in, 16)
            for h in range(NH):
                if h == 2:
                    for n in range(2):
                        sp.dma_start(rope[:, n], d["rope"][n].rearrange("(t p) c -> p t c", p=P)).then_inc(rope_in, 16)
                if h >= 2:
                    sp.wait_ge(bias_ok, h - 1)
                for qr in range(2):
                    t = d["rows"]
                    src = bass.AP(t.tensor, t.offset + (h * 15 + 1 - qr) * GRID_W * PAD_W + GRID_W - 1,
                                  [[PAD_W - 1, GRID_W], [GRID_W * PAD_W, 14], [1, GRID_W]])
                    sp.dma_start(raw[qr * GRID_W:(qr + 1) * GRID_W, h % 2], src).then_inc(raw_in[h % 2], 16)
            with nc.allow_non_contiguous_dma(reason="gain vectors by partition, once"):
                for n, name in enumerate(("na_out_g", "gqa_out_g")):
                    sp.dma_start(keep["go"][:, 4 * n:4 * n + 4], d[name][0].rearrange("(k p) -> p k", p=P)).then_inc(keep["mix_small_in"], 16)
            sp.dma_start(keep["g2"][:], d["norm2_g"].to_broadcast([P, D])).then_inc(keep["mix_small_in"], 16)
            sp.dma_start(keep["wr"][:], d["w_router"][0].rearrange("(k p) e -> p k e", p=P)).then_inc(keep["mix_small_in"], 16)
            for k in range(WO_RING):
                sp.dma_start(keep["wo32"][:, k, :], d["w_out"][0, k * P:(k + 1) * P, :]).then_inc(keep["wo_in"][k], 16)

        @block.gpsimd
        def _(pool):
            LINKS = (4, 5)
            now = [0]

            def add_masks(own, h, b, first=False):
                pool.wait_ge(raw_in[b], 32 * (h // 2 + 1) if first else 32 * (now[0] + 1))
                if not first:
                    pool.wait_ge(maxed, (h - 1) * NT + 1)
                flat = raw[:, b].rearrange("p r c -> p (r c)")
                nc.gpsimd.tensor_tensor(bias[:, b, 0:BW], flat, mask[:, 0:BW], ALU.add)
                own.link(nc.gpsimd.tensor_tensor(bias[:, b, BW:], flat[:, P:P + IW], mask[:, BW:], ALU.add))
                pool.sem_inc(bias_ok, 1)

            def columns(kind, h, kv):
                starts = (NQ0 + h * HD, NK0 + h * HD) if kind == NA else (GQ0 + h * HD, GK0 + kv * HD)
                return [proj[:, :, bass.ds(c, HD)] for c in starts]

            def prepare_na(h, b, then):
                own = Chain(pool, pool_own, LINKS[NA] * h)
                own.link(normalise_head(nc, pool, prep, own, *columns(NA, h, None), NA, h, b, False))
                pool.sem_inc(ready, 1)
                square_head(nc, pool, prep, squares, *then)
                add_masks(own, h, b)

            def prepare_gq(h, b, kv, squared=False):
                own = Chain(pool, pool_own, LINKS[NA] * NH + LINKS[GQ] * h)
                qc, kc = columns(GQ, h, kv)
                dst = qk[:, b]
                if not squared:
                    square_head(nc, pool, prep, squares, qc, kc)
                ins = normalise_head(nc, pool, prep, own, qc, kc, GQ, h + NH, b, False)
                own.link(ins)
                pairs = dst.rearrange("p t (w c two) -> p t w c two", w=2, two=2)
                sw = swp[:].rearrange("p t (w c two) -> p t w c two", w=2, two=2)
                sn = rope[:, 1].rearrange("p t (c two) -> p t c two", two=2)
                for w in range(2):
                    for o in range(2):
                        ins = nc.gpsimd.tensor_tensor(sw[:, :, w, :, o], pairs[:, :, w, :, 1 - o], sn[:, :, :, o], ALU.mult)
                own.link(ins)
                for w in range(2):
                    part = dst[:, :, w * HD:(w + 1) * HD]
                    ins = nc.gpsimd.tensor_tensor(part, part, rope[:, 0], ALU.mult)
                own.link(ins)
                nc.gpsimd.tensor_tensor(dst, dst, swp[:], ALU.add).then_inc(ready, 1)

            pool.wait_ge(mask_in, 16)
            for h in range(2):
                add_masks(Chain(pool, pool_own, 6 + h), h, h, True)
                if h == 0:
                    square_head(nc, pool, prep, squares, *columns(NA, 2, None))
            with pool.Fori(1, NH // 2 - 1) as i:
                now[0] = i
                for b in range(2):
                    prepare_na(2 * i + b, b, columns(NA, 2 * i + b + 1, None))
            now[0] = NH // 2 - 1
            prepare_na(NH - 2, 0, columns(NA, NH - 1, None))
            pool.wait_ge(rope_in, 32)
            prepare_na(NH - 1, 1, columns(GQ, 0, 0))
            for h in range(NH // KVH):
                prepare_gq(h, h % 2, 0, squared=h == 0)
            with pool.Fori(NH // 4, NH // 2) as i:
                for b in range(2):
                    prepare_gq(2 * i + b, b, 1)

        @block.tensor
        def _(pe):
            def load(b, piece, bank):
                flat = opsum[bank][:].rearrange("p t c -> p (t c)")
                for c in range(4):
                    ins = nc.tensor.transpose(flat[:, c * P:(c + 1) * P], qk[:, b, 4 * piece + c, :], ident[:])
                ins.then_inc(qk_turned, 1)

            def score(kind, h, b, t):
                g = step_of(kind, h, t)
                k0, n = tiles(kind, t)
                if not (kind == NA and isinstance(h, int) and h == 0 and t < 2):
                    pe.wait_ge(exped if kind == GQ else maxed, g)
                w = 4 * P if n != 5 else IW // 2
                for half in range(1 if n == 4 else 2):
                    cols = slice(k0 * P + half * w, k0 * P + (half + 1) * w)
                    out = spsum[t % 2][:, half, 0:w]
                    q = slice(t * P, (t + 1) * P)
                    nc.tensor.matmul(out, q1[b][:, q], k1[b][:, cols], start=True, stop=False)
                    ins = nc.tensor.matmul(out, q1[b][0:HD, q], k2[b][:, cols], start=False, stop=True)
                ins.then_inc(scored, 1)

            def turn_probs(kind, h, t):
                pe.wait_ge(exped, step_of(kind, h, t) + 2)
                k0, n = tiles(kind, t)
                for bank in range(2 if n > 4 else 1):
                    pe.wait_ge(free[bank], use(kind, h, bank, t))
                    for c in range(4 * bank, min(n, 4 * bank + 4)):
                        ins = nc.tensor.transpose(turn[bank][:, (c % 4) * P:(c % 4 + 1) * P],
                                                  prob[:, t % 2, c * P:(c + 1) * P], ident[:])
                    ins.then_inc(full[bank], 1)

            def weigh(kind, h, b, t):
                k0, n = tiles(kind, t)
                if t == 0:
                    pe.wait_ge(o_free, h + NH * kind + 1)
                for bank in range(2 if n > 4 else 1):
                    pe.wait_ge(free[bank], use(kind, h, bank, t) + 1)
                for c in range(n):
                    v = NV0 + h * HD if kind == NA else GV0 + kv_now[0] * HD
                    ins = nc.tensor.matmul(opsum[b][:, t, :], probT[t % 2][:, c * P:(c + 1) * P],
                                           proj[:, k0 + c, bass.ds(v, HD)], start=(c == 0), stop=(c == n - 1))
                ins.then_inc(summed, 1)

            def head(kind, h, b, nxt):
                j = h + NH * kind
                for t in range(NT):
                    turn_probs(kind, h, t)
                    if t == NT - 2 and nxt is not None:
                        pe.wait_ge(qk_split, 2 * j + 4)
                    to = ahead(kind, h, b, t + 2, nxt)
                    if to:
                        score(*to)
                    if t:
                        weigh(kind, h, b, t - 1)
                    if t in TURN_AT and nxt is not None:
                        if TURN_AT[t] == 0:
                            pe.wait_ge(ready, j + 2)
                            pe.wait_ge(o_free, j + 2)
                        else:
                            pe.wait_ge(qk_split, 2 * j + 3)
                        load(1 - b, TURN_AT[t], 1 - b)
                weigh(kind, h, b, NT - 1)

            kv_now = [0]
            pe.sem_inc(summed, 1)
            pe.wait_ge(ready, 1)
            for piece in range(2):
                load(0, piece, piece)
            pe.wait_ge(qk_split, 2)
            score(NA, 0, 0, 0)
            score(NA, 0, 0, 1)
            with pe.Fori(0, NH // 2 - 1) as i:
                for b in range(2):
                    head(NA, 2 * i + b, b, NA)
            head(NA, NH - 2, 0, NA)
            head(NA, NH - 1, 1, GQ)
            with pe.Fori(0, 2) as i:
                for b in range(2):
                    head(GQ, 2 * i + b, b, GQ)
            kv_now[0] = 1
            head(GQ, 4, 0, GQ)
            head(GQ, 5, 1, GQ)
            head(GQ, 6, 0, GQ)
            head(GQ, 7, 1, None)

        @block.scalar
        def _(act):
            def split_hi(b, piece, bank, n):
                act.wait_ge(qk_turned, n)
                c = slice(piece * 512, (piece + 1) * 512)
                flat = opsum[bank][:].rearrange("p t c -> p (t c)")
                nc.scalar.copy(q1[b][0:HD, c], flat[0:HD, :])
                nc.scalar.copy(k1[b][HD:P, c], flat[HD:P, :]).then_inc(hi_ok, 1)

            def exponent(kind, h, b, t):
                g = step_of(kind, h, t)
                act.wait_ge(maxed, g + 2)
                k0, n = tiles(kind, t)
                out = prob[:, t % 2, 0:n * P]
                if t >= 2 and tiles(kind, t - 2)[1] > 4:
                    act.wait_ge(full[1], use(kind, h, 1, t - 2))
                elif t < 2 and kind == GQ:
                    act.wait_ge(full[1], before(kind, h, 1) + t - 1)
                if kind == NA:
                    ins = nc.scalar.activation(out, negs[:, t % 2, 0:n * P], ACT.Exp, bias=negm[:, b, t:t + 1], scale=-1.0,
                                               accum_out=rsum[:, b, t:t + 1])
                else:
                    ins = nc.scalar.activation(out.rearrange("p (h c) -> p h c", h=2), spsum[t % 2][:], ACT.Exp,
                                               bias=negm[:, b, t:t + 1], accum_out=rsum[:, b, t:t + 1])
                ins.then_inc(exped, 1)

            def head(kind, h, b, nxt):
                j = h + NH * kind
                for t in range(NT):
                    to = ahead(kind, h, b, t + 1, nxt)
                    if to:
                        exponent(*to)
                    act.wait_ge(full[0], use(kind, h, 0, t))
                    g = step_of(kind, h, t)
                    act.wait_ge(summed, g if t else g + 1)
                    nc.scalar.copy(probT[t % 2][:, 0:4 * P], turn[0][:]).then_inc(free[0], 1)
                    if t in TURN_AT and nxt is not None:
                        split_hi(1 - b, TURN_AT[t], 1 - b, 2 * j + 3 + TURN_AT[t])

            act.sem_inc(exped, 1)
            act.sem_inc(free[0], 1)
            for piece in range(2):
                split_hi(0, piece, piece, piece + 1)
            exponent(NA, 0, 0, 0)
            heads(act, head)

        @block.vector
        def _(dve):
            dve.sem_inc(o_free, 2)
            dve.sem_inc(maxed, 1)
            dve.sem_inc(free[1], 1)
            nc_reduce = nc.vector.tensor_reduce

            def split_lo(b, piece, bank, n):
                dve.wait_ge(hi_ok, n)
                c = slice(piece * 512, (piece + 1) * 512)
                flat = opsum[bank][:].rearrange("p t c -> p (t c)")
                nc.vector.tensor_tensor(q1[b][HD:P, c], flat[0:HD, :], q1[b][0:HD, c].bitcast(F32), ALU.subtract)
                nc.vector.tensor_copy(k1[b][0:HD, c], k1[b][HD:P, c])
                nc.vector.tensor_tensor(k2[b][:, c], flat[HD:P, :], k1[b][HD:P, c].bitcast(F32), ALU.subtract).then_inc(qk_split, 1)

            def maxima(kind, h, b, t):
                g = step_of(kind, h, t)
                dve.wait_ge(scored, g + 1)
                k0, n = tiles(kind, t)
                m = negm[:, b, t:t + 1]
                if kind == GQ:
                    nc_reduce(m, spsum[t % 2][:].rearrange("p h c -> p (h c)"), AX, ALU.max, negate=True).then_inc(maxed, 1)
                    return
                if not (isinstance(h, int) and h == 0 and t < 2):
                    dve.wait_ge(exped, g)
                if t == 0:
                    dve.wait_ge(bias_ok, h + 1)
                if n == 4:
                    o = (k0 - t + 3) * P
                    s, bb, out = spsum[t % 2][:, 0, :], bias[:, b, o:o + 4 * P], negs[:, t % 2, 0:4 * P]
                else:
                    s, bb, out = (spsum[t % 2][:, :, 0:IW // 2], bias[:, b, BW:].rearrange("p (h c) -> p h c", h=2),
                                  negs[:, t % 2, :].rearrange("p (h c) -> p h c", h=2))
                dve.sem_inc(passed, 1)
                nc.vector.tensor_tensor_reduce(out=out, in0=s, in1=bb, scale=-1.0, scalar=3.0e38, op0=ALU.add,
                                               op1=ALU.min, accum_out=m).then_inc(maxed, 1)

            def head(kind, h, b, nxt):
                j = h + NH * kind
                own.base, own.n = 2 + 2 * j, 0
                sums_at = SUMS_AT[nxt if nxt is not None else kind]
                for t in range(NT):
                    k0, n = tiles(kind, t)
                    if n > 4:
                        dve.wait_ge(full[1], use(kind, h, 1, t))
                        g = step_of(kind, h, t)
                        dve.wait_ge(summed, g if t else g + 1)
                        nc.vector.tensor_copy(probT[t % 2][:, 4 * P:n * P], turn[1][:, 0:(n - 4) * P]).then_inc(free[1], 1)
                    to = ahead(kind, h, b, t + 2, nxt)
                    if to:
                        maxima(*to)
                    if t == sums_at and not (kind == GQ and isinstance(h, int) and h >= NH - 2):
                        sum_squares(nc, dve, prep, squares, own, j + 2, b)
                    elif t == sums_at:
                        own.link(nc.vector.memset(rinv[:], 1.0))
                    if t in TURN_AT and nxt is not None:
                        split_lo(1 - b, TURN_AT[t], 1 - b, 2 * j + 3 + TURN_AT[t])
                dve.wait_ge(summed, (j + 1) * NT + 1)
                own.link(nc.vector.reciprocal(rinv[:], rsum[:, b, :]))
                c0 = (GQ0 if kind == GQ else NQ0) + h * HD
                nc.vector.tensor_tensor(proj[:, :, bass.ds(c0, HD)], opsum[b][:], rinv[:].unsqueeze(2).to_broadcast([P, NT, HD]),
                                        ALU.mult).then_inc(o_free, 1)

            own = Chain(dve, dve_own)
            for piece in range(2):
                split_lo(0, piece, piece, piece + 1)
            maxima(NA, 0, 0, 0)
            maxima(NA, 0, 0, 1)
            heads(dve, head)
            dve.wait_ge(o_free, 2 * NH + 2)


def mix(nc, d, keep):
    proj, ident, affT = keep["proj"], keep["ident"], keep["affT"]
    with ExitStack() as ctx:
        sb = lambda name, shape, dt=F32: ctx.enter_context(nc.sbuf_tensor(name, shape, dt))
        ps = lambda name, shape: ctx.enter_context(nc.psum_tensor(name, shape, F32))
        sem = lambda name: ctx.enter_context(nc.semaphore(name))
        wo32 = keep["wo32"]
        woh, wol = sb("m_woh", [P, KD, D], F32R), sb("m_wol", [P, KD, D], F32R)
        go, g2, wr = keep["go"], keep["g2"], keep["wr"]
        pw = sb("m_pow", [P, 2])
        sq = sb("m_sq", [P, D])
        ss, ms, rs = sb("m_ss", [P, NT, 2]), sb("m_ms", [P, NT, 2]), sb("m_rs", [P, NT, 2])
        ss2, ms2, rs2 = sb("m_ss2", [P, NT]), sb("m_ms2", [P, NT]), sb("m_rs2", [P, NT])
        mh = [sb(f"m_mh{b}", [P, KD, P], F32R) for b in range(2)]
        ml = [sb(f"m_ml{b}", [P, KD, P], F32R) for b in range(2)]
        hn = sb("m_hn", [P, 2, D])
        hT = keep["prep"].qk[:, 0]
        nmax, den, rden = sb("m_nmax", [P, NT]), sb("m_den", [P, NT]), sb("m_rden", [P, NT])
        ex, aff = sb("m_ex", [P, E]), sb("m_aff", [P, E])
        ta = [ps(f"m_ta{b}", [P, 512]) for b in range(2)]
        tc = [ps(f"m_tc{b}", [P, 512]) for b in range(2)]
        acc = ps("m_acc", [P, 2, 512])
        lg, at = ps("m_lg", [P, 512]), ps("m_at", [P, 512])
        powc = sem("m_powc")
        small_in, wo_in = keep["mix_small_in"], keep["wo_in"]
        x_in = [sem(f"m_x_in{t}") for t in range(NT)]
        x1_out = sem("m_x1_out")
        stored = [sem(f"m_stored{b}") for b in range(2)]
        wo_hi, wo_lo = sem("m_wo_hi"), sem("m_wo_lo")
        sq_a, ms_a, rs_a, mixed, turned_a, hi_a, lo_a = (sem(f"m_{n}") for n in ("sq_a", "ms_a", "rs_a", "mixed", "turned_a", "hi_a", "lo_a"))
        multiplied, x1_ok, sq_c, ms_c, rs_c, hn_ok, turned_c, copied_c = (
            sem(f"m_{n}") for n in ("multiplied", "x1_ok", "sq_c", "ms_c", "rs_c", "hn_ok", "turned_c", "copied_c"))
        logits, maxed, exped, recip, aff_ok, aff_turned, affT_ok = (
            sem(f"m_{n}") for n in ("logits", "maxed", "exped", "recip", "aff_ok", "aff_turned", "affT_ok"))
        block = ctx.enter_context(nc.Block())
        half = lambda h: slice(512 * h, 512 * h + 512)
        x1 = lambda t: proj[:, t, NK0:NK0 + D]
        x1h = lambda t, h: proj[:, t, NK0 + 512 * h:NK0 + 512 * h + 512]
        mx = lambda t, h: proj[:, t, (NQ0, GQ0)[h]:(NQ0, GQ0)[h] + 512]

        @block.sync
        def _(sp):
            for t in range(NT):
                sp.dma_start(x1(t), d["x"][0, t * P:(t + 1) * P, :]).then_inc(x_in[t], 16)
                if t == 0:
                    for k in range(WO_RING, KD):
                        sp.wait_ge(wo_lo, k - WO_RING + 1)
                        sp.dma_start(wo32[:, k - WO_RING, :], d["w_out"][0, k * P:(k + 1) * P, :]).then_inc(wo_in[k], 16)
            for t in range(NT):
                sp.wait_ge(x1_ok, 2 * t + 2)
                sp.dma_start(d["out"][t * P:(t + 1) * P, :], x1(t)).then_inc(x1_out, 16)
                sp.wait_ge(hn_ok, t + 1)
                sp.dma_start(d["hn"][t * P:(t + 1) * P, :], hn[:, t % 2, :]).then_inc(stored[t % 2], 16)
            sp.wait_ge(x1_out, 16 * NT)
            for b in range(2):
                sp.wait_ge(stored[b], 16 * NT // 2)

        @block.gpsimd
        def _(pool):
            nc.gpsimd.memset(pw[:], -0.5)
            nc.gpsimd.memset(affT[:], 0.0).then_inc(powc, 1)
            pool.wait_ge(powc, 1)
            for t in range(-1, NT + 2):
                if t >= 2:
                    pool.wait_ge(ms_c, t - 1)
                    nc.gpsimd.tensor_tensor(rs2[:, t - 2:t - 1], ms2[:, t - 2:t - 1], pw[:, 0:1], ALU.pow).then_inc(rs_c, 1)
                if t + 1 < NT:
                    pool.wait_ge(ms_a, t + 2)
                    nc.gpsimd.tensor_tensor(rs[:, t + 1, :], ms[:, t + 1, :], pw[:], ALU.pow).then_inc(rs_a, 1)

        @block.scalar
        def _(act):
            act.wait_ge(small_in, 64)

            def squares(t):
                if t:
                    act.wait_ge(sq_a, 2 * t)
                nc.scalar.activation(sq[:, 0:512], mx(t, 0), ACT.Square, accum_out=ss[:, t, 0:1]).then_inc(sq_a, 1)
                nc.scalar.activation(sq[:, 512:1024], mx(t, 1), ACT.Square, accum_out=ss[:, t, 1:2]).then_inc(sq_a, 1)

            def stage_a(t):
                for h in range(2):
                    act.wait_ge(turned_a, 2 * t + h + 1)
                    nc.scalar.copy(mh[t % 2][:, 4 * h:4 * h + 4, :], ta[h][:].rearrange("p (k c) -> p k c", k=4)).then_inc(hi_a, 1)

            def squares_c(t):
                act.wait_ge(x1_ok, 2 * t + 2)
                if t >= 2:
                    act.wait_ge(stored[t % 2], 16 * (t // 2))
                nc.scalar.activation(hn[:, t % 2, :], x1(t), ACT.Square, accum_out=ss2[:, t:t + 1]).then_inc(sq_c, 1)

            def copies_c(t):
                for h in range(2):
                    act.wait_ge(turned_c, 2 * t + h + 1)
                    if t and h == 0:
                        act.wait_ge(logits, t)
                    nc.scalar.copy(hT[:, 4 * h:4 * h + 4, :], tc[h][:].rearrange("p (k c) -> p k c", k=4)).then_inc(copied_c, 1)

            def exponent(t):
                act.wait_ge(maxed, t + 1)
                if t:
                    act.wait_ge(aff_ok, t)
                nc.scalar.activation(ex[:], lg[:, 0:E], ACT.Exp, bias=nmax[:, t:t + 1], accum_out=den[:, t:t + 1]).then_inc(exped, 1)

            squares(0)
            for k in range(KD):
                act.wait_ge(wo_in[k], 16)
                nc.scalar.activation(woh[:, k, :], wo32[:, k % WO_RING, :], ACT.Copy, scale=go[:, k:k + 1]).then_inc(wo_hi, 1)
                if k == 1:
                    stage_a(0)
                if k == 3:
                    squares(1)
            for t in range(1, NT + 3):
                if 2 <= t <= NT + 1:
                    squares_c(t - 2)
                if t >= 3:
                    exponent(t - 3)
                if t < NT:
                    stage_a(t)
                if t + 1 < NT:
                    squares(t + 1)
                if 2 <= t <= NT + 1:
                    copies_c(t - 2)

        @block.vector
        def _(dve):
            dve.wait_ge(small_in, 64)

            def normalise(t):
                dve.wait_ge(sq_a, 2 * t + 2)
                nc.vector.tensor_scalar(ms[:, t, :], ss[:, t, :], 1.0 / 512, EPS, ALU.mult, ALU.add).then_inc(ms_a, 1)
                dve.wait_ge(rs_a, t + 1)
                for h in range(2):
                    ins = nc.vector.tensor_scalar(mx(t, h), mx(t, h), rs[:, t, h:h + 1], None, ALU.mult)
                ins.then_inc(mixed, 1)

            def stage_a(t):
                for h in range(2):
                    dve.wait_ge(hi_a, 2 * t + h + 1)
                    k = slice(4 * h, 4 * h + 4)
                    nc.vector.tensor_tensor(ml[t % 2][:, k, :], ta[h][:].rearrange("p (k c) -> p k c", k=4),
                                            mh[t % 2][:, k, :].bitcast(F32), ALU.subtract).then_inc(lo_a, 1)

            def add(t):
                dve.wait_ge(x_in[t], 16)
                for h in range(2):
                    dve.wait_ge(multiplied, 2 * t + h + 1)
                    nc.vector.tensor_tensor(x1h(t, h), acc[:, h, :], x1h(t, h), ALU.add).then_inc(x1_ok, 1)

            def normalise_c(t):
                dve.wait_ge(sq_c, t + 1)
                nc.vector.tensor_scalar(ms2[:, t:t + 1], ss2[:, t:t + 1], 1.0 / D, EPS, ALU.mult, ALU.add).then_inc(ms_c, 1)
                dve.wait_ge(rs_c, t + 1)
                dve.wait_ge(x1_ok, 2 * t + 2)
                nc.vector.scalar_tensor_tensor(out=hn[:, t % 2, :], in0=x1(t), scalar=rs2[:, t:t + 1], in1=g2[:],
                                               op0=ALU.mult, op1=ALU.mult).then_inc(hn_ok, 1)

            def route(t):
                dve.wait_ge(logits, t + 1)
                nc.vector.tensor_reduce(nmax[:, t:t + 1], lg[:, 0:E], AX, ALU.max, negate=True).then_inc(maxed, 1)
                dve.wait_ge(exped, t + 1)
                nc.vector.reciprocal(rden[:, t:t + 1], den[:, t:t + 1]).then_inc(recip, 1)
                dve.wait_ge(recip, t + 1)
                if t:
                    dve.wait_ge(aff_turned, t)
                nc.vector.tensor_scalar(aff[:], ex[:], rden[:, t:t + 1], None, ALU.mult).then_inc(aff_ok, 1)

            def keep_affinities(t):
                dve.wait_ge(aff_turned, t + 1)
                part, c = B0 * (t // (NT // 2)), t % (NT // 2) * P
                nc.vector.tensor_copy(affT[part:part + E, c:c + P], at[0:E, 0:P]).then_inc(affT_ok, 1)

            normalise(0)
            for k in range(KD):
                dve.wait_ge(wo_hi, k + 1)
                nc.vector.scalar_tensor_tensor(out=wol[:, k, :], in0=wo32[:, k % WO_RING, :], scalar=go[:, k:k + 1],
                                               in1=woh[:, k, :].bitcast(F32), op0=ALU.mult, op1=ALU.subtract).then_inc(wo_lo, 1)
                if k == 1:
                    stage_a(0)
                if k == 4:
                    normalise(1)
            for t in range(1, NT + 3):
                if 2 <= t <= NT + 1:
                    normalise_c(t - 2)
                if t >= 3:
                    route(t - 3)
                if t < NT:
                    stage_a(t)
                if t == 1:
                    add(0)
                if t + 1 < NT:
                    normalise(t + 1)
                if t >= 3:
                    keep_affinities(t - 3)
                if 2 <= t <= NT:
                    add(t - 1)
            dve.wait_ge(affT_ok, NT)

        @block.tensor
        def _(pe):
            pe.wait_ge(small_in, 64)

            def stage_a(t):
                pe.wait_ge(mixed, t + 1)
                for h in range(2):
                    if t:
                        pe.wait_ge(lo_a, 2 * t + h - 1)
                    for k in range(4):
                        ins = nc.tensor.transpose(ta[h][:, k * P:(k + 1) * P], mx(t, h)[:, k * P:(k + 1) * P], ident[:])
                    ins.then_inc(turned_a, 1)

            def stage_b(t, h):
                pe.wait_ge(lo_a, 2 * t + 2)
                pe.wait_ge(x1_ok, 2 * t + h - 1)
                for k in range(KD):
                    for m, (x, w) in enumerate(((mh, woh), (mh, wol), (ml, woh))):
                        ins = nc.tensor.matmul(acc[:, h, :], x[t % 2][:, k, :], w[:, k, half(h)],
                                               start=(k == 0 and m == 0), stop=(k == KD - 1 and m == 2))
                ins.then_inc(multiplied, 1)

            def stage_b_first():
                pe.wait_ge(lo_a, 2)
                for k in range(KD):
                    pe.wait_ge(wo_lo, k + 1)
                    for h in range(2):
                        for m, (x, w) in enumerate(((mh, woh), (mh, wol), (ml, woh))):
                            ins = nc.tensor.matmul(acc[:, h, :], x[0][:, k, :], w[:, k, half(h)],
                                                   start=(k == 0 and m == 0), stop=(k == KD - 1 and m == 2))
                        if k == KD - 1:
                            ins.then_inc(multiplied, 1)
                    if k == KD - 3:
                        stage_a(1)

            def stage_c(t):
                pe.wait_ge(hn_ok, t + 1)
                for h in range(2):
                    if t:
                        pe.wait_ge(copied_c, 2 * t + h - 1)
                    for k in range(4):
                        c = (4 * h + k) * P
                        ins = nc.tensor.transpose(tc[h][:, k * P:(k + 1) * P], hn[:, t % 2, c:c + P], ident[:])
                    ins.then_inc(turned_c, 1)

            def route(t):
                pe.wait_ge(copied_c, 2 * t + 2)
                if t:
                    pe.wait_ge(exped, t)
                for k in range(KD):
                    ins = nc.tensor.matmul(lg[:, 0:E], hT[:, k, :], wr[:, k, :], start=(k == 0), stop=(k == KD - 1))
                ins.then_inc(logits, 1)

            def turn_affinities(t):
                pe.wait_ge(aff_ok, t + 1)
                if t:
                    pe.wait_ge(affT_ok, t)
                nc.tensor.transpose(at[0:E, 0:P], aff[:], ident[:]).then_inc(aff_turned, 1)

            for t in range(NT + 3):
                if t == 1:
                    stage_b_first()
                elif 2 <= t <= NT:
                    stage_b(t - 1, 0)
                if t < NT and t != 1:
                    stage_a(t)
                if 2 <= t <= NT + 1:
                    stage_c(t - 2)
                if t >= 3:
                    turn_affinities(t - 3)
                if 2 <= t <= NT:
                    stage_b(t - 1, 1)
                if 2 <= t <= NT + 1:
                    route(t - 2)


HF = FE // 2
HT = HF // P
NGU = 4 * (KD // 2)
NDN = FE // P // 2
NCH = NGU + NDN
CW = 2 * HF
DW = 2 * D
RING = 9
SPLIT = 3
NCOL = ((0, 512), (512, 512), (1024, 384))
BATCH = ((0, 4), (4, 4), (8, 3))


def experts(nc, d, keep):
    ident, affT = keep["ident"], keep["affT"]
    with ExitStack() as ctx:
        sb = lambda name, shape, dt=F32: ctx.enter_context(nc.sbuf_tensor(name, shape, dt))
        ps = lambda name, shape: ctx.enter_context(nc.psum_tensor(name, shape, F32))
        sem = lambda name: ctx.enter_context(nc.semaphore(name))
        vals, idxs, idxf = (sb(n, [B0 + E, CAP], dt) for n, dt in (("e_vals", F32), ("e_idxs", U32), ("e_idxf", F32)))
        mval, midx, wins = (keep["squares"][0:E, S // 2 + n * CAP:S // 2 + (n + 1) * CAP] for n in range(3))
        gates, idxT = sb("e_gates", [P, E]), sb("e_idxT", [P, E], U32)
        idx = [sb(f"e_idx{b}", [P, 1], U32) for b in range(2)]
        xg = keep["squares"]
        xh, xl = sb("e_xh", [P, KD, P], F32R), sb("e_xl", [P, KD, P], F32R)
        raw = [sb(f"e_raw{s}", [P, CW]) for s in range(RING)]
        wh = [sb(f"e_wh{b}", [P, CW], F32R) for b in range(SPLIT)]
        wl = [sb(f"e_wl{b}", [P, CW], F32R) for b in range(SPLIT)]
        hid = sb("e_hid", [P, HF])
        hh, hl = sb("e_hh", [P, 2 * HT, P], F32R), sb("e_hl", [P, 2 * HT, P], F32R)
        y = xg
        acc = [ps(f"e_acc{b}", [P, 3, 512]) for b in range(2)]
        turn = [ps(f"e_turn{b}", [P, 512]) for b in range(2)]
        top, top_turned, top_ok = sem("e_top"), sem("e_top_turned"), sem("e_top_ok")
        raw_in = [sem(f"e_raw_in{s}") for s in range(RING)]
        hi_ok, lo_ok, used = sem("e_hi_ok"), sem("e_lo_ok"), sem("e_used")
        idx_ok, gathered, added = sem("e_idx_ok"), sem("e_gathered"), sem("e_added")
        x_turned = sem("e_x_turned")
        full, hi_t, lo_t = sem("e_full"), sem("e_hi_t"), sem("e_lo_t")
        y_free = sem("e_y_free")
        passed, sp_passed, first_asked = sem("e_passed"), sem("e_sp_passed"), sem("e_first_asked")
        silu_ok, hid_ok, y_ok = sem("e_silu_ok"), sem("e_hid_ok"), sem("e_y_ok")
        block = ctx.enter_context(nc.Block())

        views = {n: d[n][0].rearrange("e (c k p) f -> e c p k f", k=2, p=P) for n in ("w_gate", "w_up", "w_down")}

        def source(e, n):
            if n >= NGU:
                return views["w_down"][e, n - NGU]
            h, which, c = n // 8, n // 4 % 2, n % 4
            return views["w_up" if which else "w_gate"][e, c][:, :, h * HF:(h + 1) * HF]

        def slot(buf, n):
            w = DW if n >= NGU else CW
            return buf[:, 0:w]

        def pairs(eng, body):
            body(0, True, False)
            with eng.Fori(1, E // 2 - 1) as i:
                body(i, False, False)
            body(E // 2 - 1, False, True)

        def at_chunk(i, m, back=0):
            v = 2 * NCH * i + m + 1 - back
            return None if isinstance(i, int) and v < 1 else v

        def wait(eng, s, v):
            if v is not None:
                eng.wait_ge(s, v)

        TURNS = [(10, 0, b) for b in range(3)] + [(18, 1, b) for b in range(3)] + [(22, 2, b) for b in range(2)]
        BATCHES = {at + b: (n, half, b) for n, (at, half, b) in enumerate(TURNS)}

        def turned_to(half, b):
            if half == 2:
                return xh[:, 4 * b:4 * b + 4, :], xl[:, 4 * b:4 * b + 4, :], 4
            first, n = BATCH[b]
            t = slice(half * HT + first, half * HT + first + n)
            return hh[:, t, :], hl[:, t, :], n

        def nth_turn(i, par, n):
            return 2 + (2 * i + par) * len(TURNS) + n

        def n_of(m):
            return m % NCH

        def later(i, m, take_turn, silu=None, hidden=None, result=None):
            if m < 2:
                return later_of(i, 1, m + NCH - 2, take_turn, silu, hidden, result, back=True)
            par, n = divmod(m - 2, NCH)
            return later_of(i, par, n, take_turn, silu, hidden, result, back=False)

        def later_of(i, par, n, take_turn, silu, hidden, result, back):
            if back:
                if isinstance(i, int) and i == 0:
                    return
                i = i - 1
            if n in (3, 12) and silu:
                silu(i, par, n // 8)
            if n in (7, 15) and hidden:
                hidden(i, par, n // 8)
            if n == NCH - 1 and result:
                result(i, par)
            if n in BATCHES:
                turn_no, half, b = BATCHES[n]
                if not (half == 2 and par == 1 and isinstance(i, int) and i == E // 2 - 1):
                    take_turn(i, par, turn_no, half, b)

        @block.sync
        def _(sp):
            for m in range(RING):
                sp.dma_start(slot(raw[m], m).rearrange("p (k f) -> p k f", k=2), source(0, m)).then_inc(raw_in[m], 16)

            def body(i, first, last):
                for m in range(2 * NCH - (RING if last else 0)):
                    if first and m == 0:
                        sp.wait_ge(first_asked, 1)
                    sp.wait_ge(lo_ok, at_chunk(i, m))
                    sp.sem_inc(sp_passed, 1)
                    par, n = divmod(m + RING, NCH)
                    sp.dma_start(slot(raw[m % RING], n).rearrange("p (k f) -> p k f", k=2),
                                 source(2 * i + par, n)).then_inc(raw_in[m % RING], 16)

            pairs(sp, body)

        @block.gpsimd
        def _(pool):
            def gather(e, b, n):
                nc.gpsimd.tensor_copy(idx[b][:], idxT[:, bass.ds(e, 1)]).then_inc(idx_ok, 1)
                pool.wait_ge(idx_ok, n + 1)
                pool.sem_inc(passed, 1)
                nc.gpsimd.indirect_dma_start(out=xg[:], out_offset=None, in_=d["hn"],
                                             in_offset=bass.IndirectOffsetOnAxis(ap=idx[b][:], axis=0)).then_inc(gathered, 16)

            def body(i, first, last):
                for par in range(2):
                    e = 2 * i + par
                    if not (first and par == 0):
                        pool.wait_ge(added, 16 * e)
                        pool.sem_inc(y_free, 1)
                    if not (last and par):
                        pool.wait_ge(x_turned, e + 1)
                        gather(e + 1, 1 - par, e + 1)
                    pool.wait_ge(y_ok, e + 1)
                    pool.sem_inc(passed, 1)
                    nc.gpsimd.indirect_dma_start(out=d["out"], out_offset=bass.IndirectOffsetOnAxis(ap=idx[par][:], axis=0),
                                                 in_=y[:], in_offset=None, compute_op=ALU.add).then_inc(added, 16)

            for m in range(SPLIT):
                pool.wait_ge(hi_ok, m + 1)
                nc.gpsimd.tensor_tensor(slot(wl[m], m), slot(raw[m], m), slot(wh[m], m).bitcast(F32), ALU.subtract).then_inc(lo_ok, 1)
            pool.sem_inc(y_free, 1)
            pool.wait_ge(top_ok, 2)
            gather(0, 0, 0)
            pool.sem_inc(first_asked, 1)
            pairs(pool, body)
            pool.wait_ge(added, 16 * E)

        @block.scalar
        def _(act):
            def take_turn(i, par, n, half, b):
                hi, lo, w = turned_to(half, b)
                u = nth_turn(i, par, n)
                act.wait_ge(full, u + 1)
                nc.scalar.copy(hi, turn[n % 2][:, 0:w * P].rearrange("p (k c) -> p k c", k=w)).then_inc(hi_t, 1)

            def silu(i, par, half):
                e = 2 * i + par
                act.wait_ge(used, at_chunk(i, par * NCH + 8 * half + 3))
                if half:
                    act.wait_ge(full, nth_turn(i, par, 3))
                elif not (isinstance(i, int) and i == 0 and par == 0):
                    act.wait_ge(full, nth_turn(i, par, -2))
                nc.scalar.activation(hid[:, 0:1024], acc[par][:, 0:2, :].rearrange("p a c -> p (a c)"), ACT.Silu)
                nc.scalar.activation(hid[:, 1024:HF], acc[par][:, 2, 0:HF - 1024], ACT.Silu).then_inc(silu_ok, 1)

            def split_hi(i, m):
                act.wait_ge(raw_in[m % RING], 16 * (2 * NCH // RING * i + m // RING + 1))
                wait(act, used, at_chunk(i, m, SPLIT))
                nc.scalar.copy(slot(wh[m % SPLIT], n_of(m)), slot(raw[m % RING], n_of(m))).then_inc(hi_ok, 1)

            def body(i, first, last):
                for m in range(2 * NCH):
                    if not (first and m < SPLIT):
                        split_hi(i, m)
                    later(i, m, take_turn, silu)

            for m in range(SPLIT):
                split_hi(0, m)
            for b in range(2):
                act.wait_ge(full, b + 1)
                hi, lo, w = turned_to(2, b)
                nc.scalar.copy(hi, turn[b][:].rearrange("p (k c) -> p k c", k=w)).then_inc(hi_t, 1)
            pairs(act, body)

        @block.vector
        def _(dve):
            own = Chain(dve, top)
            for r in range(CAP // 8):
                v = vals[:, 8 * r:8 * r + 8]
                own.link(nc.vector.max(v, affT[:]))
                nc.vector.max_index(idxs[:, 8 * r:8 * r + 8], v, affT[:])
                own.link(nc.vector.match_replace(affT[:], v, affT[:], -1.0))
            own.link(nc.vector.tensor_copy(idxf[:], idxs[:]))
            backwards = lambda a: a[B0:B0 + E, ::-1]
            nc.vector.tensor_copy(mval[:], backwards(vals))
            own.link(nc.vector.tensor_scalar(midx[:], backwards(idxf), float(S // 2), None, ALU.add))
            nc.vector.tensor_tensor(wins[:], vals[0:E, :], mval[:], ALU.is_ge)
            own.link(nc.vector.tensor_tensor(idxf[0:E, :], idxf[0:E, :], midx[:], ALU.subtract))
            nc.vector.tensor_tensor(mval[:], vals[0:E, :], mval[:], ALU.max)
            own.link(nc.vector.tensor_tensor(wins[:], wins[:], idxf[0:E, :], ALU.mult))
            own.link(nc.vector.tensor_tensor(midx[:], midx[:], wins[:], ALU.add))
            dve.wait_ge(top_turned, 1)
            nc.vector.tensor_copy(gates[:], turn[0][:, 0:E]).then_inc(top_ok, 1)
            nc.vector.tensor_copy(idxT[:], turn[0][:, E:2 * E]).then_inc(top_ok, 1)
            for b in range(2):
                dve.wait_ge(hi_t, b + 1)
                hi, lo, w = turned_to(2, b)
                nc.vector.tensor_tensor(lo, turn[b][:].rearrange("p (k c) -> p k c", k=w), hi.bitcast(F32), ALU.subtract).then_inc(lo_t, 1)

            def take_turn(i, par, n, half, b):
                hi, lo, w = turned_to(half, b)
                dve.wait_ge(hi_t, nth_turn(i, par, n) + 1)
                nc.vector.tensor_tensor(lo, turn[n % 2][:, 0:w * P].rearrange("p (k c) -> p k c", k=w), hi.bitcast(F32),
                                        ALU.subtract).then_inc(lo_t, 1)

            def hidden(i, par, half):
                e = 2 * i + par
                dve.wait_ge(used, at_chunk(i, par * NCH + 8 * half + 7))
                dve.wait_ge(silu_ok, 2 * e + half + 1)
                a = acc[1 - par]
                nc.vector.tensor_tensor(hid[:, 0:1024], hid[:, 0:1024], a[:, 0:2, :].rearrange("p a c -> p (a c)"), ALU.mult)
                nc.vector.tensor_tensor(hid[:, 1024:HF], hid[:, 1024:HF], a[:, 2, 0:HF - 1024], ALU.mult).then_inc(hid_ok, 1)

            def result(i, par):
                e = 2 * i + par
                dve.wait_ge(used, at_chunk(i, par * NCH + NCH - 1))
                dve.wait_ge(y_free, e + 1)
                nc.vector.tensor_scalar(y[:], acc[par][:, 0:2, :].rearrange("p a c -> p (a c)"),
                                        gates[:, bass.ds(e, 1)], None, ALU.mult).then_inc(y_ok, 1)

            def body(i, first, last):
                for m in range(2 * NCH + 2):
                    if first and m < SPLIT:
                        pass
                    elif m < 2 * NCH:
                        dve.wait_ge(hi_ok, at_chunk(i, m))
                        nc.vector.tensor_tensor(slot(wl[m % SPLIT], n_of(m)), slot(raw[m % RING], n_of(m)),
                                                slot(wh[m % SPLIT], n_of(m)).bitcast(F32), ALU.subtract).then_inc(lo_ok, 1)
                    elif not last:
                        continue
                    else:
                        wait(dve, used, at_chunk(i, m, 2))
                    later(i, m, take_turn, None, hidden, result)

            pairs(dve, body)

        @block.tensor
        def _(pe):
            pe.wait_ge(top, 2 * CAP // 8 + 5)
            nc.tensor.transpose(turn[0][:, 0:E], mval[:], ident[0:E, 0:E])
            nc.tensor.transpose(turn[0][:, E:2 * E], midx[:], ident[0:E, 0:E]).then_inc(top_turned, 1)
            pe.wait_ge(gathered, 16)
            pe.wait_ge(top_ok, 2)
            for b in range(2):
                for k in range(4):
                    c = (4 * b + k) * P
                    ins = nc.tensor.transpose(turn[b][:, k * P:(k + 1) * P], xg[:, c:c + P], ident[:])
                ins.then_inc(full, 1)
            pe.wait_ge(full, 2)
            pe.sem_inc(x_turned, 1)

            def turn_batch(i, par, no, half, b):
                e = 2 * i + par
                u = nth_turn(i, par, no)
                if half == 2:
                    if b == 0:
                        pe.wait_ge(gathered, 16 * (e + 2))
                    for k in range(4):
                        c = (4 * b + k) * P
                        ins = nc.tensor.transpose(turn[no % 2][:, k * P:(k + 1) * P], xg[:, c:c + P], ident[:])
                else:
                    if b == 0:
                        pe.wait_ge(hid_ok, 2 * e + half + 1)
                    first, w = BATCH[b]
                    for k in range(w):
                        c = (first + k) * P
                        ins = nc.tensor.transpose(turn[no % 2][:, k * P:(k + 1) * P], hid[:, c:c + P], ident[:])
                ins.then_inc(full, 1)
                if half == 2 and b == 1:
                    pe.wait_ge(full, u + 1)
                    pe.sem_inc(x_turned, 1)

            def before_chunk(i, par, n):
                e = 2 * i + par
                if n == 0:
                    pe.wait_ge(lo_t, nth_turn(i, par, 0))
                if n == 4 and not (isinstance(i, int) and i == 0 and par == 0):
                    pe.wait_ge(y_ok, e)
                if n == 8:
                    pe.wait_ge(silu_ok, 2 * e + 1)
                if n == 12:
                    pe.wait_ge(hid_ok, 2 * e + 1)
                if n == NGU:
                    pe.wait_ge(silu_ok, 2 * e + 2)
                    pe.wait_ge(lo_t, nth_turn(i, par, 2) + 1)
                for b in range(3):
                    if n == NGU + (HT + BATCH[b][0]) // 2:
                        pe.wait_ge(lo_t, nth_turn(i, par, 3 + b) + 1)

            def body(i, first, last):
                for m in range(2 * NCH):
                    par, n = divmod(m, NCH)
                    before_chunk(i, par, n)
                    pe.wait_ge(lo_ok, at_chunk(i, m))
                    a = acc[(5 * par + (n // 4 if n < NGU else 4)) % 2]
                    for k in range(2):
                        if n < NGU:
                            kt, base, cols, ops = 2 * (n % 4) + k, k * HF, NCOL, (xh, xl)
                            start, stop = kt == 0, kt == KD - 1
                        else:
                            kt, base, cols, ops = 2 * (n - NGU) + k, k * D, ((0, 512), (512, 512)), (hh, hl)
                            start, stop = kt == 0, kt == 2 * HT - 1
                        for s, (x, w) in enumerate(((ops[0], wh), (ops[0], wl), (ops[1], wh))):
                            for c, (c0, cw) in enumerate(cols):
                                ins = nc.tensor.matmul(a[:, c, 0:cw], x[:, kt, :], w[m % SPLIT][:, base + c0:base + c0 + cw],
                                                       start=(start and s == 0), stop=(stop and s == 2))
                    ins.then_inc(used, 1)
                    if n in BATCHES:
                        turn_no, half, b = BATCHES[n]
                        if not (half == 2 and par == 1 and last):
                            if turn_no >= 0:
                                pe.wait_ge(lo_t, nth_turn(i, par, turn_no) - 1)
                            turn_batch(i, par, turn_no, half, b)

            pairs(pe, body)


def build(nc, d):
    with ExitStack() as ctx:
        keep = {
            "ident": ctx.enter_context(nc.sbuf_tensor("ident_sb", [P, P], F32)),
            "squares": ctx.enter_context(nc.sbuf_tensor("squares", [P, S], F32)),
        }
        keep["affT"] = keep["squares"][0:B0 + E, 0:S // 2]
        with ExitStack() as front:
            keep["proj"] = front.enter_context(nc.sbuf_tensor("proj", [P, NT, INW], F32))
            keep["prep"] = Prep(nc, front)
            project(nc, d, keep)
            sb = lambda name, shape: front.enter_context(nc.sbuf_tensor(name, shape, F32))
            sem = lambda name: front.enter_context(nc.semaphore(name))
            keep["wo32"], keep["go"] = sb("m_wo32", [P, WO_RING, D]), sb("m_go", [P, KD])
            keep["g2"], keep["wr"] = sb("m_g2", [P, D]), sb("m_wr", [P, KD, E])
            keep["mix_small_in"], keep["wo_in"] = sem("m_small_in"), [sem(f"m_wo_in{k}") for k in range(KD)]
            attend(nc, d, keep)
            mix(nc, d, keep)
        experts(nc, d, keep)


NAMES = ["x", "norm1_g", "w_in", "na_q_norm_g", "na_k_norm_g", "gqa_q_norm_g", "gqa_k_norm_g",
         "na_out_g", "gqa_out_g", "w_out", "norm2_g", "w_router", "w_gate", "w_up", "w_down"]


def kernel(**inputs):
    import concourse.bacc as bacc
    from concourse.bass_utils import run_bass_kernel_spmd

    arrays = {n: np.ascontiguousarray(inputs[n]) for n in NAMES}
    rpb = np.asarray(inputs["na_rpb"])[0]
    side = (PAD_W - rpb.shape[-1]) // 2
    arrays["rpb"] = np.ascontiguousarray(np.pad(rpb, ((0, 0), (0, 0), (side, side))))
    arrays.update(constants())
    nc = bacc.Bacc("TRN2", target_bir_lowering=False, num_devices=1)
    d = {n: nc.dram_tensor(f"in_{n}", a.shape, mybir.dt.from_np(a.dtype), kind="ExternalInput").ap() for n, a in arrays.items()}
    d["out"] = nc.dram_tensor("out_0", (S, D), F32, kind="ExternalOutput").ap()
    d["hn"] = nc.dram_tensor("hn", (S, D), F32, kind="Internal").ap()
    d["rows"] = nc.dram_tensor("rows", (NH, 15, GRID_W, PAD_W), F32, kind="Internal").ap()
    build(nc, d)
    got = run_bass_kernel_spmd(nc, [{f"in_{n}": a for n, a in arrays.items()}], core_ids=[0])
    return got.results[0]["out_0"].reshape(1, S, D)
```
